# Optimizing a Trainium2 kernel written in Bass

```python
import math
import jax, jax.numpy as jnp
from jax import lax
import numpy as np

D_MODEL = 1024
BATCH = 1
SEQ = 256
DEPTH = 2

N_MIXERS = 4
RMS_EPS = 1e-6
HEAD_DIM = 64
N_BUCKETS = 32
MAX_DISTANCE = 1024
N_BIAS_HEADS = D_MODEL // HEAD_DIM
POOL_WINDOWS = (2, 4, 8, 16)
N_POOL_GROUPS = len(POOL_WINDOWS)
POOL_GROUP = D_MODEL // N_POOL_GROUPS
DIL_PAIRS = ((128, 1), (512, 4), (2048, 16))
DIL_HEADS = D_MODEL // HEAD_DIM
DIFF_HEADS = D_MODEL // (2 * HEAD_DIM)
Q_BLOCK = 128
GQA_Q_HEADS = D_MODEL // HEAD_DIM
GQA_KV_HEADS = 4
GQA_WINDOW = 128
D_FF = 7 * D_MODEL // 2
N_EXPERTS = 8
TOP_K = 2

kernel_name = "hybrid_interleaved_encoder"

def _rmsnorm(x, g):
    xf = x.astype(jnp.float32)
    y = xf * lax.rsqrt(jnp.mean(xf * xf, axis=-1, keepdims=True) + RMS_EPS)
    return (y * g.astype(jnp.float32)).astype(x.dtype)

def _rel_bucket(rel):
    half = N_BUCKETS // 2
    max_exact = half // 2
    n = jnp.abs(rel)
    big = max_exact + (jnp.log(jnp.maximum(n, 1).astype(jnp.float32) / max_exact)
                       / math.log(MAX_DISTANCE / max_exact) * (half - max_exact)).astype(jnp.int32)
    big = jnp.minimum(big, half - 1)
    return jnp.where(rel > 0, half, 0) + jnp.where(n < max_exact, n, big)

def _block_len(length):
    for c in (64, 32, 16, 8):
        if length % c == 0:
            return c
    return length

def _pool_mixer(h, w_in, w_group, scale, w_out):
    b, s, _ = h.shape
    u = (h @ w_in).reshape(b, s, N_POOL_GROUPS, POOL_GROUP)
    cs = jnp.cumsum(u.astype(jnp.float32), axis=1)
    cs = jnp.concatenate([jnp.zeros_like(cs[:, :1]), cs], axis=1)
    pos = jnp.arange(s)
    pooled = []
    for g, w in enumerate(POOL_WINDOWS):
        lo = jnp.clip(pos - w // 2, 0, s)
        hi = jnp.clip(pos + (w - w // 2), 0, s)
        cnt = (hi - lo).astype(jnp.float32)
        pooled.append((cs[:, hi, g] - cs[:, lo, g]) / cnt[None, :, None])
    pooled = jnp.stack(pooled, axis=2).astype(u.dtype)
    mixed = pooled - u
    y = jnp.einsum('bsgc,gcd->bsgd', mixed, w_group).reshape(b, s, -1) * scale
    return y @ w_out

def _strided_band_attention(q, k, v, dil, half, rel_bias):
    b, s, h, c = q.shape
    L = s // dil
    qb = _block_len(L)
    nb = L // qb
    kb = qb + 2 * half

    def split(t):
        return t.reshape(b, L, dil, h, c).transpose(0, 2, 3, 1, 4)

    qs, ks, vs = split(q), split(k), split(v)
    pad = ((0, 0), (0, 0), (0, 0), (half, half), (0, 0))
    idx = jnp.arange(nb)[:, None] * qb + jnp.arange(kb)[None, :]
    kw = jnp.pad(ks, pad)[:, :, :, idx]
    vw = jnp.pad(vs, pad)[:, :, :, idx]
    qr = qs.reshape(b, dil, h, nb, qb, c)
    logits = jnp.einsum('brhnqc,brhnkc->brhnqk', qr, kw).astype(jnp.float32) * (c ** -0.5)
    rel = jnp.arange(kb)[None, :] - half - jnp.arange(qb)[:, None]
    kpos = idx - half
    valid = (jnp.abs(rel) <= half)[None] & ((kpos >= 0) & (kpos < L))[:, None, :]
    bias = rel_bias[_rel_bucket(rel * dil)].astype(jnp.float32).transpose(2, 0, 1)
    logits = jnp.where(valid, logits + bias[:, None], -jnp.inf)
    lse = jax.nn.logsumexp(logits, axis=-1)
    p = jnp.exp(logits - lse[..., None]).astype(v.dtype)
    o = jnp.einsum('brhnqk,brhnkc->brhnqc', p, vw)
    o = o.reshape(b, dil, h, L, c).transpose(0, 3, 1, 2, 4).reshape(b, s, h, c)
    lse = lse.reshape(b, dil, h, L).transpose(0, 3, 1, 2).reshape(b, s, h)
    return o, lse

def _dilated_mixer(hn, w_in, w_out, rel_bias):
    b, s, _ = hn.shape
    n_groups = len(DIL_PAIRS)
    qkv = (hn @ w_in).reshape(b, s, n_groups, 3, DIL_HEADS, HEAD_DIM)
    outs, lses = [], []
    for g, (win, dil) in enumerate(DIL_PAIRS):
        o, lse = _strided_band_attention(qkv[:, :, g, 0], qkv[:, :, g, 1], qkv[:, :, g, 2],
                                         dil, win // (2 * dil), rel_bias)
        outs.append(o)
        lses.append(lse)
    wts = jax.nn.softmax(jnp.stack(lses, axis=0), axis=0)
    o = jnp.sum(jnp.stack(outs, axis=0) * wts[..., None].astype(hn.dtype), axis=0)
    return o.reshape(b, s, -1) @ w_out

def _diff_mixer(hn, w_in, lam_vecs, subln, w_out, rel_bias, layer):
    b, s, d = hn.shape
    qkv = hn @ w_in
    q = qkv[..., :d].reshape(b, s, DIFF_HEADS, 2, HEAD_DIM)
    k = qkv[..., d:2 * d].reshape(b, s, DIFF_HEADS, 2, HEAD_DIM)
    v = qkv[..., 2 * d:].reshape(b, s, DIFF_HEADS, 2 * HEAD_DIM)
    lam_init = 0.8 - 0.6 * math.exp(-0.3 * layer)
    lv = lam_vecs.astype(jnp.float32)
    lam = jnp.exp(jnp.sum(lv[0] * lv[1])) - jnp.exp(jnp.sum(lv[2] * lv[3])) + lam_init
    scale = HEAD_DIM ** -0.5
    nq = s // Q_BLOCK
    qblocks = jnp.moveaxis(q.reshape(b, nq, Q_BLOCK, DIFF_HEADS, 2, HEAD_DIM), 1, 0)
    kpos = jnp.arange(s)

    def one_block(args):
        qblk, n = args
        rel = kpos[None, :] - (n * Q_BLOCK + jnp.arange(Q_BLOCK))[:, None]
        bias = rel_bias[_rel_bucket(rel)].astype(jnp.float32)
        bias = bias.reshape(Q_BLOCK, s, DIFF_HEADS, 2).transpose(2, 3, 0, 1)
        logits = jnp.einsum('bqhjc,bkhjc->bhjqk', qblk, k).astype(jnp.float32) * scale + bias
        p = jax.nn.softmax(logits, axis=-1)
        a = (p[:, :, 0] - lam * p[:, :, 1]).astype(v.dtype)
        return jnp.einsum('bhqk,bkhc->bqhc', a, v)

    o = lax.map(one_block, (qblocks, jnp.arange(nq)))
    o = jnp.moveaxis(o, 0, 1).reshape(b, s, DIFF_HEADS, 2 * HEAD_DIM)
    o = _rmsnorm(o, subln) * (1.0 - lam_init)
    return o.reshape(b, s, d) @ w_out

def _window_mixer(hn, w_in, sink, w_out, rel_bias):
    b, s, _ = hn.shape
    grp = GQA_Q_HEADS // GQA_KV_HEADS
    W = GQA_WINDOW
    nqc = GQA_Q_HEADS * HEAD_DIM
    nkc = GQA_KV_HEADS * HEAD_DIM
    qkv = hn @ w_in
    q = qkv[..., :nqc].reshape(b, s, GQA_KV_HEADS, grp, HEAD_DIM)
    k = qkv[..., nqc:nqc + nkc].reshape(b, s, GQA_KV_HEADS, HEAD_DIM)
    v = qkv[..., nqc + nkc:].reshape(b, s, GQA_KV_HEADS, HEAD_DIM)
    nb = s // W
    kb = 3 * W
    idx = jnp.arange(nb)[:, None] * W + jnp.arange(kb)[None, :]
    pad = ((0, 0), (W, W), (0, 0), (0, 0))
    kw = jnp.pad(k, pad)[:, idx]
    vw = jnp.pad(v, pad)[:, idx]
    qr = q.reshape(b, nb, W, GQA_KV_HEADS, grp, HEAD_DIM)
    logits = jnp.einsum('bnqhgc,bnjhc->bnhgqj', qr, kw).astype(jnp.float32) * (HEAD_DIM ** -0.5)
    rel = jnp.arange(kb)[None, :] - W - jnp.arange(W)[:, None]
    kpos = idx - W
    valid = (jnp.abs(rel) <= W)[None] & ((kpos >= 0) & (kpos < s))[:, None, :]
    bias = rel_bias[_rel_bucket(rel)].astype(jnp.float32).transpose(2, 0, 1)
    bias = bias.reshape(GQA_KV_HEADS, grp, W, kb)
    logits = jnp.where(valid[:, None, None], logits + bias, -jnp.inf)
    sk = sink.astype(jnp.float32).reshape(GQA_KV_HEADS, grp)[:, :, None, None]
    m = jnp.maximum(jnp.max(logits, axis=-1, keepdims=True), sk)
    e = jnp.exp(logits - m)
    p = e / (jnp.sum(e, axis=-1, keepdims=True) + jnp.exp(sk - m))
    o = jnp.einsum('bnhgqj,bnjhc->bnqhgc', p.astype(v.dtype), vw)
    return o.reshape(b, s, -1) @ w_out

def _swiglu(h, w_gate_up, w_down):
    gu = h @ w_gate_up
    g, u = gu[..., :D_FF], gu[..., D_FF:]
    return (jax.nn.silu(g) * u) @ w_down

def _moe(h, router, w_gate_up, w_down):
    logits = (h @ router).astype(jnp.float32)
    top_v, top_i = lax.top_k(logits, TOP_K)
    gates = jax.nn.softmax(top_v, axis=-1)
    gate_full = jnp.sum(jax.nn.one_hot(top_i, N_EXPERTS, dtype=jnp.float32) * gates[..., None], axis=-2)
    gate_full = gate_full.astype(h.dtype)
    y = jnp.zeros_like(h)
    for e in range(N_EXPERTS):
        y = y + gate_full[..., e:e + 1] * _swiglu(h, w_gate_up[e], w_down[e])
    return y

def setup_inputs(seed: int = 0) -> dict:
    key = jax.random.key(seed)
    ks = jax.random.split(key, 24)
    f32 = jnp.float32

    def nrm(k, shape, scale):
        return jax.random.normal(k, shape, f32) * scale

    n_a = len(range(0, DEPTH, N_MIXERS))
    n_b = len(range(1, DEPTH, N_MIXERS))
    n_c = len(range(2, DEPTH, N_MIXERS))
    n_d = len(range(3, DEPTH, N_MIXERS))
    n_f = len(range(0, DEPTH, 2))
    n_m = len(range(1, DEPTH, 2))
    D = D_MODEL
    n_dil = len(DIL_PAIRS)
    gqa_cols = (GQA_Q_HEADS + 2 * GQA_KV_HEADS) * HEAD_DIM
    return {
        "x": nrm(ks[0], (BATCH, SEQ, D), 1.0),
        "rel_bias": nrm(ks[1], (N_BUCKETS, N_BIAS_HEADS), 0.5),
        "norm_mix": 1.0 + nrm(ks[2], (DEPTH, D), 0.1),
        "norm_ffn": 1.0 + nrm(ks[3], (DEPTH, D), 0.1),
        "norm_final": 1.0 + nrm(ks[4], (D,), 0.1),
        "a_w_in": nrm(ks[5], (n_a, D, D), D ** -0.5),
        "a_w_group": nrm(ks[6], (n_a, N_POOL_GROUPS, POOL_GROUP, POOL_GROUP), POOL_GROUP ** -0.5),
        "a_scale": 1.0 + nrm(ks[7], (n_a, D), 0.1),
        "a_w_out": nrm(ks[8], (n_a, D, D), D ** -0.5),
        "b_w_in": nrm(ks[9], (n_b, D, n_dil * 3 * DIL_HEADS * HEAD_DIM), D ** -0.5),
        "b_w_out": nrm(ks[10], (n_b, DIL_HEADS * HEAD_DIM, D), (DIL_HEADS * HEAD_DIM) ** -0.5),
        "c_w_in": nrm(ks[11], (n_c, D, 3 * D), D ** -0.5),
        "c_lambda": nrm(ks[12], (n_c, 4, HEAD_DIM), 0.1),
        "c_subln": 1.0 + nrm(ks[13], (n_c, 2 * HEAD_DIM), 0.1),
        "c_w_out": nrm(ks[14], (n_c, D, D), D ** -0.5),
        "d_w_in": nrm(ks[15], (n_d, D, gqa_cols), D ** -0.5),
        "d_sink": nrm(ks[16], (n_d, GQA_Q_HEADS), 1.0),
        "d_w_out": nrm(ks[17], (n_d, GQA_Q_HEADS * HEAD_DIM, D), (GQA_Q_HEADS * HEAD_DIM) ** -0.5),
        "f_w_gate_up": nrm(ks[18], (n_f, D, 2 * D_FF), D ** -0.5),
        "f_w_down": nrm(ks[19], (n_f, D_FF, D), D_FF ** -0.5),
        "m_router": nrm(ks[20], (n_m, D, N_EXPERTS), D ** -0.5),
        "m_w_gate_up": nrm(ks[21], (n_m, N_EXPERTS, D, 2 * D_FF), D ** -0.5),
        "m_w_down": nrm(ks[22], (n_m, N_EXPERTS, D_FF, D), D_FF ** -0.5),
    }

def reference(x, rel_bias, norm_mix, norm_ffn, norm_final,
              a_w_in, a_w_group, a_scale, a_w_out,
              b_w_in, b_w_out,
              c_w_in, c_lambda, c_subln, c_w_out,
              d_w_in, d_sink, d_w_out,
              f_w_gate_up, f_w_down,
              m_router, m_w_gate_up, m_w_down):
    for i in range(DEPTH):
        mixer = i % N_MIXERS
        slot = i // N_MIXERS
        hn = _rmsnorm(x, norm_mix[i])
        if mixer == 0:
            y = _pool_mixer(hn, a_w_in[slot], a_w_group[slot], a_scale[slot], a_w_out[slot])
        elif mixer == 1:
            y = _dilated_mixer(hn, b_w_in[slot], b_w_out[slot], rel_bias)
        elif mixer == 2:
            y = _diff_mixer(hn, c_w_in[slot], c_lambda[slot], c_subln[slot], c_w_out[slot], rel_bias, i)
        else:
            y = _window_mixer(hn, d_w_in[slot], d_sink[slot], d_w_out[slot], rel_bias)
        x = x + y
        hn = _rmsnorm(x, norm_ffn[i])
        if i % 2 == 0:
            y = _swiglu(hn, f_w_gate_up[i // 2], f_w_down[i // 2])
        else:
            y = _moe(hn, m_router[i // 2], m_w_gate_up[i // 2], m_w_down[i // 2])
        x = x + y
    return _rmsnorm(x, norm_final)


_drawn_inputs = setup_inputs


def setup_inputs(seed=0):
    import zlib

    import numpy as np

    out = dict(_drawn_inputs(seed))
    spreads = {}
    factors = {}
    for name, (base, spread) in spreads.items():
        noise = np.random.default_rng([zlib.crc32(name.encode()), seed]).standard_normal(out[name].shape)
        drawn = base * np.exp(spread * noise) if base else spread * noise
        out[name] = __import__('jax').numpy.asarray(drawn.astype(out[name].dtype))
    for name, factor in factors.items():
        out[name] = (out[name] * factor).astype(out[name].dtype)
    return out
```

```python
from contextlib import ExitStack

import concourse.bass as bass
from concourse import mybir

P = 128
SLOTS = 4
D = 1024
S = 256
NT = S // P
KD = D // P
FF = 3584
KF = FF // P
SLABS = FF // 512
HD = 64
HEADS = 16
HH = HEADS // 2
E = 8
CAP = 128
OVER = (2 * S) // (CAP + 1)
ITEMS = E + OVER
EPS = 1e-6
SHIFT = 1000.0
BIG = 1.0e30

ALU = mybir.AluOpType
ACT = mybir.ActivationFunctionType
F32 = mybir.dt.float32
F32R = mybir.dt.float32r
I32 = mybir.dt.int32
U32 = mybir.dt.uint32

T_IN = 0
T_GROUP = 4
T_OUT = 5
T_FFN = 9
DOWN = 4 * SLABS
FFN_TILES = DOWN + 16
T_ATT = T_FFN + FFN_TILES
HALF_TILES = 20
T_MOE = T_ATT + 2 * HALF_TILES
DOWN_ROWS = [(0, 4), (4, 3), (7, 4), (11, 3), (14, 4), (18, 3), (21, 4), (25, 3)]
PAIRS0 = SLABS * NT


def encoder(nc, x_in, rel_bias, norm_mix, norm_ffn, norm_final, a_w_in, a_w_group, a_scale, a_w_out,
            b_w_in, b_w_out, f_w_gate_up, f_w_down, m_router, m_w_gate_up, m_w_down,
            c_ident, c_pool, c_bucket, c_band, c_class, c_tri, c_iota, out):
    with ExitStack() as ctx:
        sem = lambda name: ctx.enter_context(nc.semaphore(name))
        psum = lambda name: ctx.enter_context(nc.psum_tensor(name, [P, 512], F32))

        arena_bytes = (nc.sbuf_usable_end - nc.sbuf_base - 64) // 64 * 64
        arena = ctx.enter_context(nc.sbuf_tensor("arena", [P, arena_bytes // 4], F32))
        top = [nc.sbuf_base - arena_bytes]
        limit = nc.sbuf_base

        def place(name, shape, dt, parts=P):
            n = 4
            for s in shape:
                n *= s
            t = nc.alloc_sbuf_tensor_at(name, [parts] + list(shape), dt, offset=top[0])
            top[0] += (n + 31) // 32 * 32
            assert top[0] <= limit, (name, top[0] - limit)
            return t

        raw = place("raw", [SLOTS, 2048], F32)
        whi = place("whi", [SLOTS, 2048], F32R)
        wlo = place("wlo", [SLOTS, 2048], F32R)
        x = place("x", [NT, D], F32)
        gain = place("gain", [D], F32)
        xTh = place("xTh", [KD, S], F32R)
        xTl = place("xTl", [KD, S], F32R)
        ident = place("ident", [P], F32)
        band = place("band", [NT, S], F32)
        classes = place("classes", [2, P], F32)
        tri = place("tri", [2, P], F32)
        iota = place("iota", [P + 8], F32)
        scaleT = place("scaleT", [KD], F32)
        router = place("router", [KD, E], F32)
        small = place("small", [16], F32)
        ss, ms, std, rstd = (small[:, 2 * i:2 * i + 2] for i in range(4))
        nmin = place("nmin", [2, 2], F32)
        rsum = place("rsum", [2, 2], F32)
        rinv = place("rinv", [2, 2], F32)
        rank_item = place("rank_item", [NT, ITEMS + 1], F32)
        gate_item = place("gate_item", [NT, ITEMS + 1], F32)
        ids = place("ids", [16], I32)
        at_hn = top[0]
        hn = place("hn", [NT, D], F32)
        phase = top[0]
        top[0] = at_hn
        probsT = place("probsT", [2, 512], F32)

        top[0] = phase
        poolM = place("poolM", [NT, 4, S], F32)
        u = place("u", [NT, D], F32)
        mixTh = place("mixTh", [KD, S], F32R)
        mixTl = place("mixTl", [KD, S], F32R)
        yTh = place("yTh", [KD, S], F32R)
        yTl = place("yTl", [KD, S], F32R)
        bucket = place("bucket", [512], F32, parts=32)
        relb = place("relb", [HEADS], F32, parts=32)
        toep = place("toep", [512], F32, parts=HEADS)

        top[0] = phase
        dTh = place("dTh", [KF, NT, P], F32R)
        dTl = place("dTl", [KF, NT, P], F32R)
        dsilu = place("dsilu", [NT, 512], F32)
        dh = place("dh", [NT, 512], F32)

        top[0] = phase
        q = place("q", [3, 4, S], F32)
        k = place("k", [3, 4, S], F32)
        v = place("v", [NT, 3, 512], F32)
        logit = place("logit", [2, 2, 512], F32)
        oTh = place("oTh", [4, S], F32R)
        oTl = place("oTl", [4, S], F32R)
        bias = place("bias", [2, 2, 512], F32)
        biasrev = place("biasrev", [2, 2, 2, S], F32)

        top[0] = phase
        hnh = place("hnh", [NT, D], F32R)
        hnl = place("hnl", [NT, D], F32R)
        eTh = place("eTh", [KD, P], F32R)
        eTl = place("eTl", [KD, P], F32R)
        hTh = place("hTh", [KF, P], F32R)
        hTl = place("hTl", [KF, P], F32R)
        msilu = place("msilu", [512], F32)
        mh = place("mh", [512], F32)
        yh = place("yh", [D], F32R)
        yl = place("yl", [D], F32R)
        sel = place("sel", [NT, P], F32R)
        selT = place("selT", [NT, P], F32R)
        routh = place("routh", [KD, E], F32R)
        routl = place("routl", [KD, E], F32R)
        tiny = place("tiny", [16, 16], F32)
        idx = place("idx", [NT, 8], U32)

        G, U, T, X, Y0, Y1, S0, S1 = (psum(n) for n in ("bG", "bU", "bT", "bX", "bY0", "bY1", "bS0", "bS1"))
        toep_dram = nc.dram_tensor("toeplitz", (HEADS, 512), F32, kind="Internal").ap()

        x_in_done = sem("x_in_done")
        c_in = [sem(f"const{i}") for i in range(10)]
        raw_full = [sem(f"raw_full{i}") for i in range(SLOTS)]
        hi_done, lo_done, tile_used = sem("hi_done"), sem("lo_done"), sem("tile_used")
        chain = sem("chain")
        gain_full = sem("gain_full")
        ms_done, std_done, hn_done = sem("ms_done"), sem("std_done"), sem("hn_done")
        tx_psum, tx_hi, tx_lo = sem("tx_psum"), sem("tx_hi"), sem("tx_lo")
        u_act, u_dve = sem("u_act"), sem("u_dve")
        mix_psum, mix_hi, mix_lo = sem("mix_psum"), sem("mix_hi"), sem("mix_lo")
        grp_psum, grp_hi, grp_lo = sem("grp_psum"), sem("grp_hi"), sem("grp_lo")
        toep_psum, toep_sb, toep_out = sem("toep_psum"), sem("toep_sb"), sem("toep_out")
        silu_done, h_ready = sem("silu_done"), sem("h_ready")
        ht_psum, ht_hi, ht_lo = sem("ht_psum"), sem("ht_hi"), sem("ht_lo")
        pj_first, pj_act, pj_dve = sem("pj_first"), sem("pj_act"), sem("pj_dve")
        rev_full = [sem("rev_full0"), sem("rev_full1")]
        bias_ready = sem("bias_ready")
        qk_done, logit_done, exp_done, prob_done = sem("qk_done"), sem("logit_done"), sem("exp_done"), sem("prob_done")
        pT_psum, pT_act, pT_dve = sem("pT_psum"), sem("pT_act"), sem("pT_dve")
        pv_done, o_hi, o_lo = sem("pv_done"), sem("o_hi"), sem("o_lo")
        hnh_done, hnl_done = sem("hnh_done"), sem("hnl_done")
        rt_hi, rt_lo = sem("rt_hi"), sem("rt_lo")
        logits_psum, gap_done, e_done, sel_ready = sem("logits_psum"), sem("gap_done"), sem("e_done"), sem("sel_ready")
        rank_psum, ids_ready = sem("rank_psum"), sem("ids_ready")
        pick_ready = sem("pick_ready")
        ga_psum, ga_act, ga_dve = sem("ga_psum"), sem("ga_act"), sem("ga_dve")
        selT_psum, selT_ready = sem("selT_psum"), sem("selT_ready")
        y_hi, y_lo, sc_psum, x_added = sem("y_hi"), sem("y_lo"), sem("sc_psum"), sem("x_added")
        out_ready, stored = sem("out_ready"), sem("stored")

        CONST = [
            (ident[:], c_ident), (poolM[:], c_pool.rearrange("(t p) g s -> p t g s", p=P)),
            (scaleT[:], a_scale),
            (bucket[:], c_bucket), (relb[:], rel_bias),
            (band[:], c_band.rearrange("(t p) s -> p t s", p=P)),
            (classes[:], c_class.rearrange("c p s -> p c s")), (tri[:], c_tri.rearrange("c p s -> p c s")),
            (iota[:], c_iota.partition_broadcast(P)), (router[:], m_router[0].rearrange("(k p) e -> p k e", p=P)),
        ]
        C_IDENT, C_POOL, C_SCALE, C_BUCKET, C_RELB, C_BAND, C_CLASS, C_TRI, C_IOTA, C_ROUTER = range(10)
        GAINS = [norm_mix[0], norm_ffn[0], norm_mix[1], norm_ffn[1], norm_final]

        def ffn_tile(gate_up, down, t):
            if t < DOWN:
                j, part, kh = t // 4, t % 4 // 2, t % 2
                c = part * FF + j * 512
                return gate_up[kh * 512:kh * 512 + 512, c:c + 512], 4
            n, (k0, nk) = (t - DOWN) // 8, DOWN_ROWS[(t - DOWN) % 8]
            return down[k0 * P:(k0 + nk) * P, n * 512:n * 512 + 512], nk

        def tile_source(t):
            if t < T_GROUP:
                return a_w_in[0][t % 2 * 512:t % 2 * 512 + 512, t // 2 * 512:t // 2 * 512 + 512], 4
            if t < T_FFN:
                t -= T_OUT
                return a_w_out[0][t % 2 * 512:t % 2 * 512 + 512, t // 2 * 512:t // 2 * 512 + 512], 4
            if t < T_ATT:
                return ffn_tile(f_w_gate_up[0], f_w_down[0], t - T_FFN)
            if t < T_MOE:
                half, s = divmod(t - T_ATT, HALF_TILES)
                if s < 18:
                    c = s // 2 * 1024 + half * 512
                    return b_w_in[0][s % 2 * 512:s % 2 * 512 + 512, c:c + 512], 4
                return b_w_out[0][half * 512:half * 512 + 512, (s - 18) * 512:(s - 17) * 512], 4
            return ffn_tile(m_w_gate_up[0, 0], m_w_down[0, 0], t - T_MOE)

        def blocks(t):
            if t == T_GROUP:
                return 4
            if t >= T_MOE:
                return ffn_tile(m_w_gate_up[0, 0], m_w_down[0, 0], (t - T_MOE) % FFN_TILES)[1]
            return tile_source(t)[1]

        def slot(t):
            return t % SLOTS

        def rows(t):
            return 512 * blocks(t)

        def make_hi(act, t, item=0):
            s = slot(t)
            act.wait_ge(raw_full[s], item * (16 * (FFN_TILES // SLOTS)) + 16 * (t // SLOTS + 1))
            if t >= SLOTS:
                act.wait_ge(tile_used, item * FFN_TILES + t - SLOTS + 1)
            nc.scalar.activation(whi[:, s, :rows(t)], raw[:, s, :rows(t)], ACT.Copy).then_inc(hi_done, 1)

        def make_lo(dve, t, item=0):
            s = slot(t)
            dve.wait_ge(hi_done, item * FFN_TILES + t + 1)
            if t >= SLOTS:
                dve.wait_ge(tile_used, item * FFN_TILES + t - SLOTS + 1)
            nc.vector.tensor_tensor(wlo[:, s, :rows(t)], raw[:, s, :rows(t)],
                                    whi[:, s, :rows(t)].bitcast(F32), ALU.subtract).then_inc(lo_done, 1)

        def wblk(t, b):
            s = slot(t)
            return whi[:, s, b * 512:b * 512 + 512], wlo[:, s, b * 512:b * 512 + 512]

        def mm3(pe, dst, a, b, start, stop):
            pe.matmul(dst, a[0], b[0], start=start, stop=False)
            pe.matmul(dst, a[1], b[0], start=False, stop=False)
            return pe.matmul(dst, a[0], b[1], start=False, stop=stop)

        def tok(h, l, kb, tb):
            return h[:, kb, tb * P:tb * P + P], l[:, kb, tb * P:tb * P + P]

        block = ctx.enter_context(nc.Block())

        @block.sync
        def _(sp):
            for a in range(4):
                sp.dma_start(x[a % 2 * 64:a % 2 * 64 + 64, a // 2, :],
                             x_in[0].rearrange("(m a) d -> a m d", a=4)[a]).then_inc(x_in_done, 16)

            def load(t, item=0, src=None):
                s = slot(t)
                if t >= SLOTS:
                    sp.wait_ge(lo_done, item * FFN_TILES + t - SLOTS + 1)
                if t == T_GROUP:
                    sp.dma_start(raw[:, s, :].rearrange("p (b n) -> p b n", n=256),
                                 a_w_group[0].rearrange("g (c p) n -> p (g c) n", p=P)).then_inc(raw_full[s], 16)
                    return
                if src is None:
                    src = tile_source(t)[0]
                sp.dma_start(raw[:, s, :rows(t)].rearrange("p (k n) -> p k n", n=512),
                             src.rearrange("(k p) n -> p k n", p=P)).then_inc(raw_full[s], 16)

            for t in range(T_MOE + SLOTS):
                load(t)

            def item_tiles(i, e, e_next):
                gu, dn = m_w_gate_up[0, bass.ds(e, 1)], m_w_down[0, bass.ds(e, 1)]
                gu, dn = gu.rearrange("o k n -> (o k) n"), dn.rearrange("o k n -> (o k) n")
                for t in range(SLOTS, FFN_TILES):
                    load(T_MOE + t, i, ffn_tile(gu, dn, t)[0])
                gu = m_w_gate_up[0, bass.ds(e_next, 1)].rearrange("o k n -> (o k) n")
                for t in range(SLOTS):
                    load(T_MOE + FFN_TILES + t, i, ffn_tile(gu, dn, t)[0])

            with sp.Fori(0, E - 1) as i:
                item_tiles(i, i, i + 1)
            sp.wait_ge(ids_ready, 1)
            n_items = sp.value_load(ids[0:1, 0:1], min_val=E, max_val=ITEMS)
            with sp.Fori(E - 1, ITEMS) as i:
                with sp.If(i < n_items):
                    e = sp.value_load(ids[0:1, bass.ds(i - (E - 2), 1)], min_val=0, max_val=E - 1)
                    e_next = sp.value_load(ids[0:1, bass.ds(i - (E - 3), 1)], min_val=0, max_val=E - 1)
                    item_tiles(i, e, e_next)
                with sp.Else():
                    sp.nop()

            for a in range(4):
                if a % 2 == 0:
                    sp.wait_ge(out_ready, a // 2 + 1)
                sp.dma_start(out[0].rearrange("(m a) d -> a m d", a=4)[a],
                             hn[a % 2 * 64:a % 2 * 64 + 64, a // 2, :]).then_inc(stored, 16)
            sp.wait_ge(stored, 64)

        @block.gpsimd
        def _(pool):
            def load_gain(n):
                if n >= 1:
                    pool.wait_ge(hn_done, 2 * n)
                pool.dma_start(gain[:], GAINS[n].partition_broadcast(P)).then_inc(gain_full, 16)

            load_gain(0)
            pool.wait_ge(toep_sb, 1)
            pool.dma_start(toep_dram, toep[:]).then_inc(toep_out, 16)
            pool.wait_ge(toep_out, 16)
            load_gain(1)
            load_gain(2)
            pool.wait_ge(hn_done, 6)
            pool.wait_ge(c_in[C_BAND], 16)
            pool.wait_ge(c_in[C_CLASS], 16)

            def load_rev(c):
                if c >= 2:
                    pool.wait_ge(bias_ready, 2 * (c - 1))
                for a in range(4):
                    src = bass.AP(toep_dram.tensor, 2 * c * 512 + a, [[4, 64], [512, 2], [1, S]])
                    pool.dma_start(biasrev[a % 2 * 64:a % 2 * 64 + 64, c % 2, a // 2], src).then_inc(rev_full[c % 2], 16)

            load_rev(0)
            load_rev(1)
            per_part = 2 * 2 * 2 * S
            for h in range(HEADS):
                c = h // 2
                if h % 2 == 0:
                    pool.wait_ge(rev_full[c % 2], 64 * (c // 2 + 1))
                if h >= 2:
                    pool.wait_ge(logit_done, h - 1)
                for qt in range(2):
                    base = ((c % 2 * 2 + qt) * 2 + h % 2) * S + S - 1
                    rev = lambda a0, na: bass.AP(biasrev[:].tensor, base - a0, [[per_part, P], [-1, na], [-4, 64]])
                    to = bias[:, h % 2, qt]
                    nc.gpsimd.tensor_tensor(to[:, 0:S].rearrange("p (a m) -> p a m", a=4), rev(0, 4),
                                            band[:, qt].rearrange("p (a m) -> p a m", a=4), ALU.add)
                    for g in range(2):
                        last = nc.gpsimd.tensor_tensor(
                            to[:, S + g * P:S + g * P + P].rearrange("p (a m) -> p a m", a=2), rev(2 * qt, 2),
                            classes[:, g].rearrange("p (a m) -> p a m", a=2), ALU.add)
                last.then_inc(bias_ready, 1)
                if h % 2 == 1 and c + 2 < HEADS // 2:
                    load_rev(c + 2)
                if h == 3:
                    load_gain(3)
            load_gain(4)

        @block.tensor
        def _(pe):
            def tile_ready(t, item=0):
                pe.wait_ge(lo_done, item * FFN_TILES + t + 1)

            def transpose_x(n):
                pe.wait_ge(hn_done, 2 * n + 2)
                for b, bank in enumerate((G, U, T, X)):
                    for kk in range(2):
                        for tb in range(NT):
                            mm = pe.transpose(bank[:, kk * S + tb * P:kk * S + tb * P + P],
                                              hn[:, tb, (2 * b + kk) * P:(2 * b + kk + 1) * P], ident[:])
                    mm.then_inc(tx_psum, 1)

            def dense(t0, xh, xl, kbs, banks, wait=True):
                done = 0
                for n, ks in enumerate(kbs):
                    tile_ready(t0 + n)
                    for tb in range(NT):
                        for b, kb in enumerate(ks):
                            mm = mm3(pe, banks[tb][:], tok(xh, xl, kb, tb), wblk(t0 + n, b),
                                     start=done + b == 0, stop=n == len(kbs) - 1 and b == len(ks) - 1)
                    done += len(ks)
                    mm.then_inc(tile_used, 1)

            pe.wait_ge(c_in[C_BUCKET], 16)
            pe.wait_ge(c_in[C_RELB], 16)
            pe.matmul(S0[0:HEADS, :], relb[:], bucket[:], start=True, stop=True).then_inc(toep_psum, 1)

            pe.wait_ge(c_in[C_IDENT], 16)
            transpose_x(0)
            pe.wait_ge(tx_lo, 4)
            for n in range(2):
                dense(T_IN + 2 * n, xTh, xTl, [range(0, 4), range(4, 8)], ((G, U), (Y0, Y1))[n])
            pe.wait_ge(u_act, 2)
            pe.wait_ge(u_dve, 2)
            pe.wait_ge(c_in[C_POOL], 16)
            pe.wait_ge(toep_sb, 1)
            for b, bank in enumerate((T, X, S0, S1)):
                for kk in range(2):
                    cb = 2 * b + kk
                    for tb in range(NT):
                        mm = pe.matmul(bank[:, kk * S:kk * S + S], u[:, tb, cb * P:cb * P + P],
                                       poolM[:, tb, cb // 2, :], start=tb == 0, stop=tb == NT - 1)
                mm.then_inc(mix_psum, 1)
            tile_ready(T_GROUP)
            for g, bank in enumerate((G, U, Y0, Y1)):
                pe.wait_ge(mix_lo, g + 1)
                for db in range(2):
                    for cb in range(2):
                        c = g * 512 + cb * S + db * P
                        w = whi[:, slot(T_GROUP), c:c + P], wlo[:, slot(T_GROUP), c:c + P]
                        r = mixTh[:, 2 * g + cb, :], mixTl[:, 2 * g + cb, :]
                        mm = mm3(pe, bank[:, db * S:db * S + S], w, r, start=cb == 0, stop=cb == 1)
                mm.then_inc(*((tile_used, 1) if g == 3 else (grp_psum, 1)))
            for g in range(4):
                pe.wait_ge(grp_lo, g + 1)
            for n in range(2):
                dense(T_OUT + 2 * n, yTh, yTl, [range(0, 4), range(4, 8)], ((T, X), (S0, S1))[n])

            transpose_x(1)
            pe.wait_ge(tx_lo, 8)

            def turn_hidden(j, width, src, ready):
                pe.wait_ge(h_ready, ready)
                for tb in range(width):
                    for c in range(4):
                        mm = pe.transpose((T, X)[tb][:, c * P:c * P + P], src(tb)[:, c * P:c * P + P], ident[:])
                    mm.then_inc(ht_psum, 1)

            for j in range(SLABS):
                t = T_FFN + 4 * j
                if j >= 1:
                    pe.wait_ge(silu_done, NT * j)
                dense(t, xTh, xTl, [range(0, 4), range(4, 8)], (G, S0))
                if j >= 1:
                    if j >= 2:
                        pe.wait_ge(ht_lo, NT * (j - 1))
                    turn_hidden(j - 1, NT, lambda tb: dh[:, tb], NT * j)
                dense(t + 2, xTh, xTl, [range(0, 4), range(4, 8)], (U, S1))
            down = [range(k0, k0 + nk) for k0, nk in DOWN_ROWS]
            acc = (Y0, Y1), (S0, S1)
            for n in range(2):
                for qn, ks in enumerate(down):
                    t = T_FFN + DOWN + 8 * n + qn
                    if n == 0 and qn == 0:
                        pe.wait_ge(ht_lo, NT * (SLABS - 1))
                    if n == 0 and qn == 6:
                        pe.wait_ge(ht_lo, NT * SLABS)
                    tile_ready(t)
                    for tb in range(NT):
                        for b, kb in enumerate(ks):
                            mm = mm3(pe, acc[n][tb][:], (dTh[:, kb, tb], dTl[:, kb, tb]), wblk(t, b),
                                     start=kb == 0, stop=kb == KF - 1)
                    mm.then_inc(tile_used, 1)
                    if n == 0 and qn == 0:
                        turn_hidden(SLABS - 1, NT, lambda tb: dh[:, tb], NT * SLABS)

            transpose_x(2)
            pe.wait_ge(tx_lo, 12)
            for half in range(2):
                t0 = T_ATT + half * HALF_TILES
                for s in range(9):
                    n = half * 9 + s
                    banks = ((G, U), (Y0, Y1))[s % 2]
                    if s >= 2:
                        pe.wait_ge(pj_act, n - 1)
                        pe.wait_ge(pj_dve, n - 1)
                    if s % 3 == 2:
                        dense(t0 + 2 * s, xTh, xTl, [range(0, 4), range(4, 8)], banks)
                        continue
                    tile_ready(t0 + 2 * s + 1)
                    for cb in range(4):
                        for kb in range(KD):
                            h_, l_ = wblk(t0 + 2 * s + kb // 4, kb % 4)
                            mm = mm3(pe, banks[cb // 2][:, cb % 2 * S:cb % 2 * S + S],
                                     (h_[:, cb * P:cb * P + P], l_[:, cb * P:cb * P + P]),
                                     (xTh[:, kb], xTl[:, kb]), start=kb == 0, stop=kb == KD - 1)
                            if cb == 3 and kb % 4 == 3:
                                mm.then_inc(tile_used, 1)
                        if cb == 1:
                            mm.then_inc(pj_first, 1)

                def scores(h):
                    head = half * HH + h
                    r = h % 2 * HD
                    if h == 0:
                        pe.wait_ge(pj_act, 9 * half + 9)
                        pe.wait_ge(pj_dve, 9 * half + 9)
                    if h >= 2:
                        pe.wait_ge(logit_done, head - 1)
                    for qt in range(2):
                        bank = ((G, U), (Y0, Y1))[h % 2][qt]
                        for g in range(3):
                            cols = slice(0, S) if g == 0 else slice(qt * P, qt * P + P)
                            to = slice(0, S) if g == 0 else slice(S + (g - 1) * P, S + g * P)
                            mm = pe.matmul(bank[:, to], q[r:r + HD, g, h // 2, qt * P:qt * P + P],
                                           k[r:r + HD, g, h // 2, cols], start=True, stop=True)
                    mm.then_inc(qk_done, 1)

                scores(0)
                scores(1)
                for h in range(HH):
                    head = half * HH + h
                    pe.wait_ge(prob_done, head + 1)
                    for qt in range(2):
                        for c in range(4):
                            mm = pe.transpose((T, X)[qt][:, c * P:c * P + P], logit[:, h % 2, qt, c * P:c * P + P], ident[:])
                    mm.then_inc(pT_psum, 1)
                    if h + 2 < HH:
                        scores(h + 2)
                    o = (S0, S1)[h // 2 % 2]
                    r = h % 2 * HD
                    pe.wait_ge(pT_act, head + 1)
                    pe.wait_ge(pT_dve, head + 1)
                    if h % 2 == 0 and head >= 4:
                        pe.wait_ge(o_lo, head // 2 - 1)
                    for kt in range(NT):
                        pe.matmul(o[r:r + HD, 0:S].rearrange("p (a b) -> p a b", a=2), v[:, kt, 0, h * HD:h * HD + HD],
                                  probsT[:, :, kt * P:kt * P + P], start=kt == 0, stop=False, skip_group_check=True)
                    for qt in range(2):
                        for g in (1, 2):
                            mm = pe.matmul(o[r:r + HD, qt * P:qt * P + P], v[:, qt, g, h * HD:h * HD + HD],
                                           probsT[:, qt, S + (g - 1) * P:S + g * P], start=False,
                                           stop=g == 2, skip_group_check=True)
                    mm.then_inc(pv_done, 1)
                pe.wait_ge(o_lo, 4 * half + 4)
                for n in range(2):
                    dense(t0 + 18 + n, oTh, oTl, [range(0, 4)], ((T, X), (S0, S1))[n])

            transpose_x(3)
            pe.wait_ge(tx_lo, 16)
            pe.wait_ge(rt_lo, 1)
            for tb in range(NT):
                for kb in range(KD):
                    mm = mm3(pe, Y0[:, tb * E:tb * E + E], tok(xTh, xTl, kb, tb), (routh[:, kb], routl[:, kb]),
                             start=kb == 0, stop=kb == KD - 1)
            mm.then_inc(logits_psum, 1)
            pe.wait_ge(c_in[C_TRI], 16)
            pe.wait_ge(sel_ready, 1)
            chosen = tiny[:, 4, :]
            pe.matmul(Y1[:, 0:E], tri[:, 0], chosen[:, 0:E], start=True, stop=True)
            pe.matmul(Y1[:, E:2 * E], tri[:, 1], chosen[:, 0:E], start=True, stop=False)
            pe.matmul(Y1[:, E:2 * E], tri[:, 0], chosen[:, E:2 * E], start=False, stop=True)
            pe.matmul(Y1[:, 2 * E:3 * E], tri[:, 1], chosen[:, 0:E], start=True, stop=False)
            pe.matmul(Y1[:, 2 * E:3 * E], tri[:, 1], chosen[:, E:2 * E], start=False, stop=True).then_inc(rank_psum, 1)

            def gather(n):
                pe.wait_ge(pick_ready, n + 1)
                for r, bank in enumerate((G, U, T, X)):
                    src = (hnh, hnl)[r // 2]
                    for kk in range(4):
                        kb = r % 2 * 4 + kk
                        for tb in range(NT):
                            mm = pe.matmul(bank[:, kk * P:kk * P + P], src[:, tb, kb * P:kb * P + P], sel[:, tb, :],
                                           start=tb == 0, stop=tb == NT - 1)
                    mm.then_inc(ga_psum, 1)

            def turn_sel(n):
                for tb in range(NT):
                    mm = pe.transpose(Y0[:, tb * P:tb * P + P], sel[:, tb, :].bitcast(F32), ident[:])
                mm.then_inc(selT_psum, 1)

            pe.wait_ge(hnl_done, 2)
            gather(0)
            turn_sel(0)
            pe.wait_ge(ids_ready, 1)
            n_items = pe.value_load(ids[0:1, 0:1], min_val=E, max_val=ITEMS)

            def item_body(i):
                pe.wait_ge(ga_act, i * 2 + 2)
                pe.wait_ge(ga_dve, i * 2 + 2)

                def product(t, xh, xl, ks, bank, first, last):
                    tile_ready(T_MOE + t, i)
                    for b, kb in enumerate(ks):
                        mm = mm3(pe, bank[:], (xh[:, kb], xl[:, kb]), wblk(T_MOE + t, b), start=kb == 0 and first,
                                 stop=last and b == len(ks) - 1)
                    mm.then_inc(tile_used, 1)

                for j in range(SLABS):
                    if j >= 1:
                        pe.wait_ge(silu_done, i * SLABS + PAIRS0 + j)
                    product(4 * j, eTh, eTl, range(0, 4), G, True, False)
                    product(4 * j + 1, eTh, eTl, range(4, 8), G, True, True)
                    if j >= 1:
                        pe.wait_ge(ht_lo, i * SLABS + PAIRS0 + j - 1)
                        turn_hidden(j - 1, 1, lambda tb: mh[:], i * SLABS + PAIRS0 + j)
                    product(4 * j + 2, eTh, eTl, range(0, 4), U, True, False)
                    product(4 * j + 3, eTh, eTl, range(4, 8), U, True, True)
                for n in range(2):
                    bank = (Y0, Y1)[n]
                    for qn, ks in enumerate(down):
                        if n == 0 and qn == 0:
                            pe.wait_ge(ht_lo, i * SLABS + PAIRS0 + SLABS - 1)
                            pe.wait_ge(selT_ready, i + 1)
                        if n == 0 and qn == 6:
                            pe.wait_ge(ht_lo, i * SLABS + PAIRS0 + SLABS)
                        product(DOWN + 8 * n + qn, hTh, hTl, ks, bank, True, qn == 7)
                        if n == 0 and qn == 0:
                            turn_hidden(SLABS - 1, 1, lambda tb: mh[:], i * SLABS + PAIRS0 + SLABS)
                        if n == 1 and qn == 1:
                            spread(i, 0)
                gather(i + 1)
                spread(i, 1)
                turn_sel(i + 1)

            def spread(i, n):
                pe.wait_ge(y_lo, i * 2 + n + 1)
                pe.wait_ge(x_added, i * 2 + n + 1)
                for tb in range(NT):
                    bank = (S0, S1)[tb]
                    pe.matmul(bank[:], selT[:, tb], yh[:, n * 512:n * 512 + 512], start=True, stop=False)
                    mm = pe.matmul(bank[:], selT[:, tb], yl[:, n * 512:n * 512 + 512], start=False, stop=True)
                mm.then_inc(sc_psum, 1)

            with pe.Fori(0, ITEMS) as i:
                with pe.If(i < n_items):
                    item_body(i)
                with pe.Else():
                    pe.nop()

        @block.scalar
        def _(act):
            for n, (dst, src) in enumerate(CONST):
                act.dma_start(dst, src).then_inc(c_in[n], 16)

            def copy(dst, src, s, scale=1.0):
                return nc.scalar.activation(dst, src, ACT.Copy, scale=scale).then_inc(s, 1)

            def root(n):
                act.wait_ge(ms_done, n + 1)
                nc.scalar.activation(std, ms, ACT.Sqrt).then_inc(std_done, 1)

            def cut_x(n):
                for b, bank in enumerate((G, U, T, X)):
                    act.wait_ge(tx_psum, 4 * n + b + 1)
                    copy(xTh[:, 2 * b:2 * b + 2, :].rearrange("p k s -> p (k s)"), bank[:], tx_hi)

            root(0)
            make_hi(act, 0)
            cut_x(0)
            for t in range(1, SLOTS):
                make_hi(act, t)
            act.wait_ge(toep_psum, 1)
            copy(toep[:], S0[0:HEADS, :], toep_sb, scale=-1.0)
            for n in range(2):
                make_hi(act, 2 * n + SLOTS)
                act.wait_ge(tile_used, 2 * n + 2)
                copy(u[:, 0, n * 512:n * 512 + 512], ((G, Y0)[n])[:], u_act)
                make_hi(act, 2 * n + 1 + SLOTS)
            for b, bank in enumerate((T, X, S0, S1)):
                act.wait_ge(mix_psum, b + 1)
                copy(mixTh[:, 2 * b:2 * b + 2, :].rearrange("p k s -> p (k s)"), bank[:], mix_hi)
            act.wait_ge(c_in[C_SCALE], 16)
            for g, bank in enumerate((G, U, Y0, Y1)):
                if g < 3:
                    act.wait_ge(grp_psum, g + 1)
                else:
                    act.wait_ge(tile_used, T_GROUP + 1)
                for db in range(2):
                    last = nc.scalar.activation(yTh[:, 2 * g + db, :], bank[:, db * S:db * S + S], ACT.Copy,
                                                scale=scaleT[:, 2 * g + db:2 * g + db + 1])
                last.then_inc(grp_hi, 1)
            for t in range(T_GROUP, T_FFN):
                make_hi(act, t + SLOTS)

            act.wait_ge(toep_out, 16)
            root(1)
            cut_x(1)
            for j in range(SLABS):
                t = T_FFN + 4 * j
                make_hi(act, t + SLOTS)
                for tb in range(NT):
                    act.wait_ge(tile_used, t + 2)
                    if j >= 1:
                        act.wait_ge(h_ready, NT * j)
                    nc.scalar.activation(dsilu[:, tb], (G, S0)[tb][:], ACT.Silu).then_inc(silu_done, 1)
                make_hi(act, t + 1 + SLOTS)
                if j >= 1:
                    for tb in range(NT):
                        act.wait_ge(ht_psum, NT * (j - 1) + tb + 1)
                        copy(dTh[:, 4 * j - 4:4 * j, tb], (T, X)[tb][:].rearrange("p (c t) -> p c t", c=4), ht_hi)
                make_hi(act, t + 2 + SLOTS)
                make_hi(act, t + 3 + SLOTS)
            for t in range(DOWN, FFN_TILES):
                make_hi(act, T_FFN + t + SLOTS)
                if t == DOWN:
                    for tb in range(NT):
                        act.wait_ge(ht_psum, NT * (SLABS - 1) + tb + 1)
                        copy(dTh[:, KF - 4:KF, tb], (T, X)[tb][:].rearrange("p (c t) -> p c t", c=4), ht_hi)

            root(2)
            cut_x(2)
            for half in range(2):
                t0 = T_ATT + half * HALF_TILES
                for s in range(9):
                    g, kind = divmod(s, 3)
                    bank = ((G, U), (Y0, Y1))[s % 2][0]
                    if kind < 2:
                        act.wait_ge(pj_first, half * 6 + 2 * g + kind + 1)
                        copy((q, k)[kind][:, g, 0:2].rearrange("p c s -> p (c s)"), bank[:], pj_act,
                             scale=-0.125 if kind == 0 else 1.0)
                        make_hi(act, t0 + 2 * s + SLOTS)
                    else:
                        make_hi(act, t0 + 2 * s + SLOTS)
                        act.wait_ge(tile_used, t0 + 2 * s + 2)
                        copy(v[:, 0, g], bank[:], pj_act)
                    make_hi(act, t0 + 2 * s + 1 + SLOTS)

                def exps(h):
                    act.wait_ge(logit_done, half * HH + h + 1)
                    for qt in range(2):
                        last = nc.scalar.activation(logit[:, h % 2, qt], logit[:, h % 2, qt], ACT.Exp, scale=-1.0,
                                                    bias=nmin[:, h % 2, qt:qt + 1], accum_out=rsum[:, h % 2, qt:qt + 1])
                    last.then_inc(exp_done, 1)

                exps(0)
                for h in range(HH):
                    head = half * HH + h
                    if h + 1 < HH:
                        exps(h + 1)
                    act.wait_ge(pT_psum, head + 1)
                    if head >= 1:
                        act.wait_ge(pv_done, head)
                    copy(probsT[:, 0], T[:], pT_act)
                    if h % 2 == 1:
                        act.wait_ge(pv_done, head + 1)
                        copy(oTh[:, h // 2], (S0, S1)[h // 2 % 2][:, 0:S], o_hi)
                for n in range(2):
                    make_hi(act, t0 + 18 + n + SLOTS)

            root(3)
            act.wait_ge(c_in[C_ROUTER], 16)
            copy(routh[:], router[:], rt_hi)
            cut_x(3)
            for tb in range(NT):
                copy(hnh[:, tb], hn[:, tb], hnh_done)
            act.wait_ge(gap_done, 1)
            nc.scalar.activation(tiny[:, 1, 0:2], tiny[:, 0, 0:2], ACT.Exp).then_inc(e_done, 1)

            def cut_tokens(n):
                for r, bank in enumerate((G, U)):
                    act.wait_ge(ga_psum, 4 * n + r + 1)
                    copy(eTh[:, 4 * r:4 * r + 4].rearrange("p k t -> p (k t)"), bank[:], ga_act)

            def copy_selT(n):
                act.wait_ge(selT_psum, n + 1)
                copy(selT[:].rearrange("p t s -> p (t s)"), Y0[:, 0:S], selT_ready)

            cut_tokens(0)
            copy_selT(0)
            act.wait_ge(ids_ready, 1)
            n_items = act.value_load(ids[0:1, 0:1], min_val=E, max_val=ITEMS)

            def item_body(i):
                def ahead(t):
                    make_hi(act, T_MOE + t + SLOTS, i)

                def hidden_hi(j):
                    act.wait_ge(ht_psum, i * SLABS + PAIRS0 + j + 1)
                    copy(hTh[:, 4 * j:4 * j + 4].rearrange("p c t -> p (c t)"), T[:], ht_hi)

                def y_cut(n):
                    act.wait_ge(tile_used, i * FFN_TILES + T_MOE + DOWN + 8 * n + 8)
                    copy(yh[:, n * 512:n * 512 + 512], (Y0, Y1)[n][:], y_hi)

                for j in range(SLABS):
                    ahead(4 * j)
                    act.wait_ge(tile_used, i * FFN_TILES + T_MOE + 4 * j + 2)
                    act.wait_ge(h_ready, i * SLABS + PAIRS0 + j)
                    nc.scalar.activation(msilu[:], G[:], ACT.Silu).then_inc(silu_done, 1)
                    ahead(4 * j + 1)
                    if j >= 1:
                        hidden_hi(j - 1)
                    ahead(4 * j + 2)
                    ahead(4 * j + 3)
                for t in range(DOWN, FFN_TILES):
                    ahead(t)
                    if t == DOWN:
                        hidden_hi(SLABS - 1)
                    if t == DOWN + 7:
                        y_cut(0)
                y_cut(1)
                cut_tokens(i + 1)
                copy_selT(i + 1)

            with act.Fori(0, ITEMS) as i:
                with act.If(i < n_items):
                    item_body(i)
                with act.Else():
                    act.nop()
            root(4)

        @block.vector
        def _(dve):
            links = [0]

            def link(ins):
                links[0] += 1
                ins.then_inc(chain, 1)
                dve.wait_ge(chain, links[0])

            def norm(n, done):
                for tb in range(NT):
                    last = nc.vector.tensor_tensor_reduce(hn[:, tb], x[:, tb], x[:, tb], 1.0, 0.0, ALU.mult, ALU.add,
                                                          accum_out=ss[:, tb:tb + 1])
                link(last)
                nc.vector.tensor_scalar(ms, ss, 1.0 / D, EPS, ALU.mult, ALU.add).then_inc(ms_done, 1)
                dve.wait_ge(std_done, n + 1)
                link(nc.vector.reciprocal(rstd, std))
                dve.wait_ge(gain_full, 16 * (n + 1))
                for tb in range(NT):
                    ins = nc.vector.scalar_tensor_tensor(hn[:, tb], x[:, tb], rstd[:, tb:tb + 1], gain[:], ALU.mult, ALU.mult)
                    ins.then_inc(done, 1)

            def lo(dst, src, hi, s):
                return nc.vector.tensor_tensor(dst, src, hi.bitcast(F32), ALU.subtract).then_inc(s, 1)

            def cut_x(n):
                for b, bank in enumerate((G, U, T, X)):
                    dve.wait_ge(tx_hi, 4 * n + b + 1)
                    f = lambda t: t[:, 2 * b:2 * b + 2, :].rearrange("p k s -> p (k s)")
                    lo(f(xTl), bank[:], f(xTh), tx_lo)

            def add_x(n, banks):
                for tb in range(NT):
                    sl = x[:, tb, n * 512:n * 512 + 512]
                    last = nc.vector.tensor_tensor(sl, banks[tb][:], sl, ALU.add)
                link(last)

            dve.wait_ge(x_in_done, 64)
            norm(0, hn_done)
            make_lo(dve, 0)
            cut_x(0)
            for t in range(1, SLOTS):
                make_lo(dve, t)
            for n in range(2):
                make_lo(dve, 2 * n + SLOTS)
                dve.wait_ge(tile_used, 2 * n + 2)
                nc.vector.tensor_copy(u[:, 1, n * 512:n * 512 + 512], ((U, Y1)[n])[:]).then_inc(u_dve, 1)
                make_lo(dve, 2 * n + 1 + SLOTS)
            for b, bank in enumerate((T, X, S0, S1)):
                dve.wait_ge(mix_hi, b + 1)
                f = lambda t: t[:, 2 * b:2 * b + 2, :].rearrange("p k s -> p (k s)")
                lo(f(mixTl), bank[:], f(mixTh), mix_lo)
            for g, bank in enumerate((G, U, Y0, Y1)):
                dve.wait_ge(grp_hi, g + 1)
                for db in range(2):
                    last = nc.vector.scalar_tensor_tensor(
                        yTl[:, 2 * g + db], bank[:, db * S:db * S + S], scaleT[:, 2 * g + db:2 * g + db + 1],
                        yTh[:, 2 * g + db].bitcast(F32), ALU.mult, ALU.subtract)
                last.then_inc(grp_lo, 1)
            for t in range(T_GROUP, T_FFN):
                make_lo(dve, t + SLOTS)
            for n in range(2):
                dve.wait_ge(tile_used, T_OUT + 2 * n + 2)
                add_x(n, ((T, X), (S0, S1))[n])

            norm(1, hn_done)
            cut_x(1)
            for j in range(SLABS):
                t = T_FFN + 4 * j
                make_lo(dve, t + SLOTS)
                make_lo(dve, t + 1 + SLOTS)
                if j >= 1:
                    for tb in range(NT):
                        dve.wait_ge(ht_hi, NT * (j - 1) + tb + 1)
                        lo(dTl[:, 4 * j - 4:4 * j, tb], (T, X)[tb][:].rearrange("p (c t) -> p c t", c=4),
                           dTh[:, 4 * j - 4:4 * j, tb], ht_lo)
                make_lo(dve, t + 2 + SLOTS)
                dve.wait_ge(tile_used, t + 4)
                for tb in range(NT):
                    dve.wait_ge(silu_done, NT * j + tb + 1)
                    if j >= 1:
                        dve.wait_ge(ht_psum, NT * j)
                    nc.vector.tensor_tensor(dh[:, tb], (U, S1)[tb][:], dsilu[:, tb], ALU.mult).then_inc(h_ready, 1)
                make_lo(dve, t + 3 + SLOTS)
            for t in range(DOWN, FFN_TILES):
                make_lo(dve, T_FFN + t + SLOTS)
                if t == DOWN:
                    for tb in range(NT):
                        dve.wait_ge(ht_hi, NT * (SLABS - 1) + tb + 1)
                        lo(dTl[:, KF - 4:KF, tb], (T, X)[tb][:].rearrange("p (c t) -> p c t", c=4),
                           dTh[:, KF - 4:KF, tb], ht_lo)
                if t == DOWN + 7:
                    dve.wait_ge(tile_used, T_FFN + t + 1)
                    add_x(0, (Y0, Y1))
            dve.wait_ge(tile_used, T_ATT)
            add_x(1, (S0, S1))

            norm(2, hn_done)
            cut_x(2)
            for half in range(2):
                t0 = T_ATT + half * HALF_TILES
                for s in range(9):
                    g, kind = divmod(s, 3)
                    bank = ((G, U), (Y0, Y1))[s % 2][1]
                    make_lo(dve, t0 + 2 * s + SLOTS)
                    dve.wait_ge(tile_used, t0 + 2 * s + 2)
                    if kind == 0:
                        nc.vector.tensor_scalar(q[:, g, 2:4].rearrange("p c s -> p (c s)"), bank[:], -0.125, None,
                                                ALU.mult).then_inc(pj_dve, 1)
                    else:
                        to = k[:, g, 2:4].rearrange("p c s -> p (c s)") if kind == 1 else v[:, 1, g]
                        nc.vector.tensor_copy(to, bank[:]).then_inc(pj_dve, 1)
                    make_lo(dve, t0 + 2 * s + 1 + SLOTS)

                def logits(h):
                    head = half * HH + h
                    dve.wait_ge(qk_done, head + 1)
                    dve.wait_ge(bias_ready, head + 1)
                    for qt in range(2):
                        last = nc.vector.tensor_tensor_reduce(
                            logit[:, h % 2, qt], ((G, U), (Y0, Y1))[h % 2][qt][:], bias[:, h % 2, qt], 1.0, 3.0e38,
                            ALU.add, ALU.min, accum_out=nmin[:, h % 2, qt:qt + 1])
                    last.then_inc(logit_done, 1)

                logits(0)
                logits(1)
                for h in range(HH):
                    head = half * HH + h
                    dve.wait_ge(exp_done, head + 1)
                    link(nc.vector.reciprocal(rinv[:, h % 2], rsum[:, h % 2]))
                    for qt in range(2):
                        last = nc.vector.tensor_scalar(logit[:, h % 2, qt], logit[:, h % 2, qt],
                                                       rinv[:, h % 2, qt:qt + 1], None, ALU.mult)
                    last.then_inc(prob_done, 1)
                    dve.wait_ge(pT_psum, head + 1)
                    if head >= 1:
                        dve.wait_ge(pv_done, head)
                    nc.vector.tensor_copy(probsT[:, 1], X[:]).then_inc(pT_dve, 1)
                    if h + 2 < HH:
                        logits(h + 2)
                    if h % 2 == 1:
                        dve.wait_ge(o_hi, head // 2 + 1)
                        lo(oTl[:, h // 2], (S0, S1)[h // 2 % 2][:, 0:S], oTh[:, h // 2], o_lo)
                for n in range(2):
                    make_lo(dve, t0 + 18 + n + SLOTS)
                for n in range(2):
                    dve.wait_ge(tile_used, t0 + 18 + n + 1)
                    add_x(n, ((T, X), (S0, S1))[n])

            norm(3, hn_done)
            dve.wait_ge(rt_hi, 1)
            lo(routl[:], router[:], routh[:], rt_lo)
            cut_x(3)
            for tb in range(NT):
                dve.wait_ge(hnh_done, tb + 1)
                lo(hnl[:, tb], hn[:, tb], hnh[:, tb], hnl_done)
            gap, ex, gates, chosen, picked, gatev = (tiny[:, i, :] for i in (0, 1, 2, 4, 5, 6))
            logs, best, idxf = tiny[:, 7, :], tiny[:, 8, :], tiny[:, 9, 0:4]
            place_, over_place, full, kth, mask = (tiny[:, i, :] for i in (10, 11, 12, 13, 14))
            junk, eid = tiny[:, 15, 0:8], tiny[:, 3, :]
            two = lambda t: t.rearrange("p (t e) -> p t e", e=E)
            dve.wait_ge(logits_psum, 1)
            link(nc.vector.tensor_copy(logs, Y0[:, 0:2 * E]))
            for tb in range(NT):
                link(nc.vector.max(best[:, tb * 8:tb * 8 + 8], logs[:, tb * 8:tb * 8 + 8]))
            nc.vector.tensor_tensor(gap[:, 0:2], two(best)[:, :, 1], two(best)[:, :, 0], ALU.subtract).then_inc(gap_done, 1)
            for tb in range(NT):
                link(nc.vector.max_index(idx[:, tb], best[:, tb * 8:tb * 8 + 8], logs[:, tb * 8:tb * 8 + 8]))
            link(nc.vector.tensor_copy(idxf.rearrange("p (t c) -> p t c", c=2), idx[:, :, 0:2]))
            dve.wait_ge(c_in[C_IOTA], 16)
            first, second = picked, gatev
            for tb in range(NT):
                sl = slice(tb * 8, tb * 8 + 8)
                nc.vector.tensor_scalar(first[:, sl], iota[:, P:P + 8], idxf[:, 2 * tb:2 * tb + 1], None, ALU.is_equal)
                last = nc.vector.tensor_scalar(second[:, sl], iota[:, P:P + 8], idxf[:, 2 * tb + 1:2 * tb + 2], None, ALU.is_equal)
            link(last)
            nc.vector.tensor_tensor(chosen, first, second, ALU.add).then_inc(sel_ready, 1)
            dve.wait_ge(sel_ready, 1)
            dve.wait_ge(e_done, 1)
            link(nc.vector.tensor_scalar(gates[:, 0:2], ex[:, 0:2], 1.0, None, ALU.add))
            link(nc.vector.reciprocal(gates[:, 2:4], gates[:, 0:2]))
            link(nc.vector.tensor_tensor(gates[:, 4:6], ex[:, 0:2], gates[:, 2:4], ALU.mult))
            for tb in range(NT):
                sl = slice(tb * 8, tb * 8 + 8)
                link(nc.vector.tensor_scalar(junk, first[:, sl], gates[:, 2 + tb:3 + tb], None, ALU.mult))
                link(nc.vector.scalar_tensor_tensor(gate_item[:, tb, 0:E], second[:, sl], gates[:, 4 + tb:5 + tb], junk,
                                                    ALU.mult, ALU.add))
            dve.wait_ge(rank_psum, 1)
            for tb in range(NT):
                sl = slice(tb * 8, tb * 8 + 8)
                nc.vector.scalar_tensor_tensor(rank_item[:, tb, 0:E], Y1[:, sl], SHIFT, chosen[:, sl], ALU.add, ALU.mult)
                last = nc.vector.scalar_tensor_tensor(over_place[:, sl], Y1[:, sl], SHIFT - CAP, chosen[:, sl],
                                                      ALU.add, ALU.mult)
            link(last)

            def pick(n):
                for tb in range(NT):
                    last = nc.vector.tensor_scalar(sel[:, tb], iota[:, 0:P], rank_item[:, tb, bass.ds(n, 1)], None, ALU.is_equal)
                last.then_inc(pick_ready, 1)

            pick(0)
            nc.vector.memset(kth, 0.0)
            nc.vector.memset(full, 0.0)
            link(nc.vector.memset(mask, 0.0))
            link(nc.vector.tensor_scalar(full[:, 8:16], Y1[:, 16:24], float(CAP), None, ALU.is_gt))
            link(nc.vector.tensor_tensor(kth[:, 8:16], full[:, 8:16], full[:, 7:15], ALU.add))
            link(nc.vector.tensor_tensor(mask[:, 8:16], kth[:, 8:16], kth[:, 6:14], ALU.add))
            link(nc.vector.tensor_tensor(kth[:, 8:16], mask[:, 8:16], mask[:, 4:12], ALU.add))
            link(nc.vector.tensor_scalar(eid[:, 0:1], kth[:, 15:16], float(E), None, ALU.add))
            link(nc.vector.tensor_tensor(kth[:, 0:8], kth[:, 8:16], full[:, 8:16], ALU.mult))
            nc.vector.memset(eid[:, 2 + OVER:3 + OVER], 0.0)
            link(nc.vector.memset(eid[:, 1:2], float(E - 1)))
            for n in range(OVER):
                link(nc.vector.tensor_scalar(mask[:, 0:8], kth[:, 0:8], float(n + 1), None, ALU.is_equal))
                link(nc.vector.tensor_tensor_reduce(junk, mask[:, 0:8], iota[:, P:P + 8], 1.0, 0.0, ALU.mult, ALU.add,
                                                    accum_out=eid[:, 2 + n:3 + n]))
                for tb in range(NT):
                    sl = slice(tb * 8, tb * 8 + 8)
                    link(nc.vector.tensor_tensor_reduce(junk, mask[:, 0:8], over_place[:, sl], 1.0, 0.0, ALU.mult, ALU.add,
                                                        accum_out=rank_item[:, tb, E + n:E + n + 1]))
                    link(nc.vector.tensor_tensor_reduce(junk, mask[:, 0:8], gate_item[:, tb, 0:E], 1.0, 0.0, ALU.mult, ALU.add,
                                                        accum_out=gate_item[:, tb, E + n:E + n + 1]))
            nc.vector.memset(rank_item[:, :, ITEMS:ITEMS + 1], 0.0).then_inc(x_added, 1)
            nc.vector.tensor_copy(ids[:, 0:3 + OVER], eid[:, 0:3 + OVER]).then_inc(ids_ready, 1)

            def tokens_lo(n):
                for r, bank in enumerate((T, X)):
                    dve.wait_ge(ga_psum, 4 * n + r + 3)
                    nc.vector.tensor_copy(eTl[:, 4 * r:4 * r + 4].rearrange("p k t -> p (k t)"), bank[:]).then_inc(ga_dve, 1)

            tokens_lo(0)
            dve.wait_ge(ids_ready, 1)
            n_items = dve.value_load(ids[0:1, 0:1], min_val=E, max_val=ITEMS)

            def item_body(i):
                def ahead(t):
                    make_lo(dve, T_MOE + t + SLOTS, i)

                def hidden_lo(j):
                    dve.wait_ge(ht_hi, i * SLABS + PAIRS0 + j + 1)
                    f = lambda t: t[:, 4 * j:4 * j + 4].rearrange("p c t -> p (c t)")
                    lo(f(hTl), T[:], f(hTh), ht_lo)

                def y_cut(n):
                    dve.wait_ge(y_hi, i * 2 + n + 1)
                    sl = slice(n * 512, n * 512 + 512)
                    lo(yl[:, sl], (Y0, Y1)[n][:], yh[:, sl], y_lo)

                def add_item(n):
                    dve.wait_ge(sc_psum, i * 2 + n + 1)
                    dve.wait_ge(x_added, i * 2 + n + 1)
                    for tb in range(NT):
                        sl = x[:, tb, n * 512:n * 512 + 512]
                        last = nc.vector.scalar_tensor_tensor(sl, (S0, S1)[tb][:], gate_item[:, tb, bass.ds(i, 1)], sl,
                                                              ALU.mult, ALU.add)
                    last.then_inc(x_added, 1)

                for j in range(SLABS):
                    ahead(4 * j)
                    ahead(4 * j + 1)
                    if j >= 1:
                        hidden_lo(j - 1)
                    if j == 1:
                        dve.wait_ge(selT_psum, i + 1)
                        pick(i + 1)
                    ahead(4 * j + 2)
                    dve.wait_ge(tile_used, i * FFN_TILES + T_MOE + 4 * j + 4)
                    dve.wait_ge(silu_done, i * SLABS + PAIRS0 + j + 1)
                    dve.wait_ge(ht_psum, i * SLABS + PAIRS0 + j)
                    nc.vector.tensor_tensor(mh[:], U[:], msilu[:], ALU.mult).then_inc(h_ready, 1)
                    ahead(4 * j + 3)
                for t in range(DOWN, FFN_TILES):
                    ahead(t)
                    if t == DOWN:
                        hidden_lo(SLABS - 1)
                    if t == DOWN + 7:
                        y_cut(0)
                    if t == DOWN + 11:
                        add_item(0)
                y_cut(1)
                tokens_lo(i + 1)
                add_item(1)

            with dve.Fori(0, ITEMS) as i:
                with dve.If(i < n_items):
                    item_body(i)
                with dve.Else():
                    dve.nop()
            dve.wait_ge(x_added, n_items * 2 + 1)
            norm(4, out_ready)


def constants():
    import numpy as np
    pos = np.array([4 * (p % 64) + p // 64 for p in range(S)])
    pool = np.zeros((S, 4, S), np.float32)
    for g, w in enumerate((2, 4, 8, 16)):
        lo = np.clip(pos - w // 2, 0, S)
        hi = np.clip(pos + w - w // 2, 0, S)
        inside = (pos[:, None] >= lo[None]) & (pos[:, None] < hi[None])
        pool[:, g] = inside / (hi - lo)[None].astype(np.float64) - (pos[:, None] == pos[None])
    rel = S - 1 - np.arange(512)
    n = np.abs(rel)
    big = 8 + (np.log(np.maximum(n, 1) / 8.0) / np.log(1024 / 8.0) * 8).astype(np.int32)
    b = np.where(rel > 0, 16, 0) + np.where(n < 8, n, np.minimum(big, 15))
    bucket = (np.arange(32)[:, None] == b[None]).astype(np.float32)
    d = pos[None] - pos[:, None]
    band = np.where(np.abs(d) <= 64, 0.0, BIG).astype(np.float32)
    same = d[:P, :P]
    classes = np.stack([np.where(same % m == 0, 0.0, BIG) for m in (4, 16)]).astype(np.float32)
    tri = np.stack([np.arange(P)[:, None] < np.arange(P)[None], np.ones((P, P))]).astype(np.float32)
    slots = np.where(np.arange(P) < CAP, np.arange(P) + SHIFT, -1.0)
    iota = np.concatenate([slots, np.arange(8)]).astype(np.float32)
    return {"ident": np.eye(P, dtype=np.float32), "pool": pool, "bucket": bucket, "band": band,
            "class": classes, "tri": tri, "iota": iota}


_INS = ["x", "rel_bias", "norm_mix", "norm_ffn", "norm_final", "a_w_in", "a_w_group", "a_scale", "a_w_out",
        "b_w_in", "b_w_out", "f_w_gate_up", "f_w_down", "m_router", "m_w_gate_up", "m_w_down"]


def kernel(**inputs):
    import numpy as _np
    import concourse.bacc as _bacc
    from concourse import mybir as _mybir
    from concourse.bass_utils import run_bass_kernel_spmd as _run

    nc = _bacc.Bacc("TRN2", target_bir_lowering=False, num_devices=1)
    data = {n: _np.ascontiguousarray(inputs[n]) for n in _INS}
    data["a_scale"] = _np.ascontiguousarray(data["a_scale"].reshape(KD, P).T)
    data.update({f"const_{n}": a for n, a in constants().items()})
    arrays, args = {}, []
    for name, a in data.items():
        arrays[f"in_{name}_dram"] = a
        args.append(nc.dram_tensor(f"in_{name}_dram", a.shape, _mybir.dt.from_np(a.dtype), kind="ExternalInput").ap())
    args.append(nc.dram_tensor("out_0_dram", (1, S, D), _mybir.dt.float32, kind="ExternalOutput").ap())
    encoder(nc, *args)
    r = _run(nc, [arrays], core_ids=[0])
    return r.results[0]["out_0_dram"]
```

```python
from contextlib import ExitStack

import concourse.bass as bass
from concourse import mybir

P = 128
RAW = 7
CUT = 3
D = 1024
S = 256
NT = S // P
KD = D // P
FF = 3584
KF = FF // P
SLABS = FF // 512
HD = 64
HEADS = 16
HH = HEADS // 2
E = 8
CAP = 128
OVER = (2 * S) // (CAP + 1)
ITEMS = E + OVER
EPS = 1e-6
SHIFT = 1000.0
BIG = 1.0e30

ALU = mybir.AluOpType
ACT = mybir.ActivationFunctionType
F32 = mybir.dt.float32
F32R = mybir.dt.float32r
I32 = mybir.dt.int32
U32 = mybir.dt.uint32

T_IN = 0
T_GROUP = 4
T_OUT = 5
T_FFN = 9
DOWN = 4 * SLABS
DT = KF // 4
FFN_TILES = DOWN + 2 * DT
T_ATT = T_FFN + FFN_TILES
HALF_TILES = 20
T_MOE = T_ATT + 2 * HALF_TILES
PAIRS0 = SLABS * NT


def encoder(nc, x_in, rel_bias, gains_t, norm_ffn, norm_final, a_w_in, a_w_group, a_scale, a_w_out,
            b_w_in, b_w_out, f_w_gate_up, f_w_down, m_router, m_w_gate_up, m_w_down,
            c_ident, c_pool, c_bucket, c_band, c_class, c_tri, c_iota, out):
    with ExitStack() as ctx:
        sem = lambda name: ctx.enter_context(nc.semaphore(name))
        psum = lambda name: ctx.enter_context(nc.psum_tensor(name, [P, 512], F32))

        arena_bytes = (nc.sbuf_usable_end - nc.sbuf_base - 64) // 64 * 64
        arena = ctx.enter_context(nc.sbuf_tensor("arena", [P, arena_bytes // 4], F32))
        top = [nc.sbuf_base - arena_bytes]
        limit = nc.sbuf_base

        def place(name, shape, dt, parts=P):
            n = 4
            for s in shape:
                n *= s
            t = nc.alloc_sbuf_tensor_at(name, [parts] + list(shape), dt, offset=top[0])
            top[0] += (n + 31) // 32 * 32
            assert top[0] <= limit, (name, top[0] - limit)
            return t

        raw = place("raw", [RAW, 2048], F32)
        whi = place("whi", [CUT, 2048], F32R)
        wlo = place("wlo", [CUT, 2048], F32R)
        x = place("x", [NT, D], F32)
        gain = place("gain", [2, D], F32)
        gainT = place("gainT", [4, KD], F32)
        xTh = place("xTh", [KD, S], F32R)
        xTl = place("xTl", [KD, S], F32R)
        ident = place("ident", [P], F32)
        band = place("band", [NT, S], F32)
        classes = place("classes", [2, P], F32)
        tri = place("tri", [2, P], F32)
        iota = place("iota", [P + 8], F32)
        scaleT = place("scaleT", [KD], F32)
        router = place("router", [KD, E], F32)
        routh = place("routh", [KD, E], F32R)
        routl = place("routl", [KD, E], F32R)
        rdiag = place("rdiag", [NT, P], F32)
        rcols = place("rcols", [S], F32)
        small = place("small", [16], F32)
        ss, ms, std, rstd = (small[:, 2 * i:2 * i + 2] for i in range(4))
        nmin = place("nmin", [2, 2], F32)
        rsum = place("rsum", [2, 2], F32)
        rinv = place("rinv", [2, 2], F32)
        rank_item = place("rank_item", [NT, ITEMS + 1], F32)
        gate_item = place("gate_item", [NT, ITEMS + 1], F32)
        ids = place("ids", [16], I32)
        at_hn = top[0]
        hn = place("hn", [NT, D], F32)
        phase = top[0]
        top[0] = at_hn
        probsT = place("probsT", [2, 512], F32)

        top[0] = phase
        poolM = place("poolM", [NT, 4, S], F32)
        u = place("u", [NT, D], F32)
        mixTh = place("mixTh", [KD, S], F32R)
        mixTl = place("mixTl", [KD, S], F32R)
        yTh = place("yTh", [KD, S], F32R)
        yTl = place("yTl", [KD, S], F32R)
        bucket = place("bucket", [512], F32, parts=32)
        relb = place("relb", [HEADS], F32, parts=32)
        toep = place("toep", [512], F32, parts=HEADS)

        top[0] = phase
        dTh = place("dTh", [KF, NT, P], F32R)
        dTl = place("dTl", [KF, NT, P], F32R)
        dsilu = place("dsilu", [NT, 512], F32)
        dh = place("dh", [NT, 512], F32)

        top[0] = phase
        q = place("q", [3, 4, S], F32)
        k = place("k", [3, 4, S], F32)
        v = place("v", [NT, 3, 512], F32)
        logit = place("logit", [2, 2, 512], F32)
        oTh = place("oTh", [4, S], F32R)
        oTl = place("oTl", [4, S], F32R)
        bias = place("bias", [2, 2, 512], F32)
        biasrev = place("biasrev", [2, 2, 2, S], F32)

        top[0] = phase
        hnh = place("hnh", [NT, D], F32R)
        hnl = place("hnl", [NT, D], F32R)
        eTh = place("eTh", [KD, P], F32R)
        eTl = place("eTl", [KD, P], F32R)
        hTh = place("hTh", [KF, P], F32R)
        hTl = place("hTl", [KF, P], F32R)
        msilu = place("msilu", [512], F32)
        mh = place("mh", [512], F32)
        yh = place("yh", [D], F32R)
        yl = place("yl", [D], F32R)
        sel = place("sel", [NT, P], F32R)
        selT = place("selT", [NT, P], F32R)
        tiny = place("tiny", [16, 16], F32)
        idx = place("idx", [NT, 8], U32)

        G, U, T, X, Y0, Y1, S0, S1 = (psum(n) for n in ("bG", "bU", "bT", "bX", "bY0", "bY1", "bS0", "bS1"))
        toep_dram = nc.dram_tensor("toeplitz", (HEADS, 512), F32, kind="Internal").ap()

        x_in_done = sem("x_in_done")
        c_in = [sem(f"const{i}") for i in range(13)]
        raw_full = [sem(f"raw_full{i}") for i in range(RAW)]
        hi_done, lo_done, tile_used = sem("hi_done"), sem("lo_done"), sem("tile_used")
        chain = sem("chain")
        ms_done, std_done, hn_done = sem("ms_done"), sem("std_done"), sem("hn_done")
        rstd_done, x_sum = sem("rstd_done"), sem("x_sum")
        rdiag_done, rcols_psum, rcols_done = sem("rdiag_done"), sem("rcols_psum"), sem("rcols_done")
        tx_psum, tx_hi, tx_lo = sem("tx_psum"), sem("tx_hi"), sem("tx_lo")
        u_act, u_dve = sem("u_act"), sem("u_dve")
        mix_psum, mix_hi, mix_lo = sem("mix_psum"), sem("mix_hi"), sem("mix_lo")
        grp_psum, grp_hi, grp_lo = sem("grp_psum"), sem("grp_hi"), sem("grp_lo")
        toep_psum, toep_sb, toep_out = sem("toep_psum"), sem("toep_sb"), sem("toep_out")
        silu_done, h_ready = sem("silu_done"), sem("h_ready")
        ht_psum, ht_hi, ht_lo = sem("ht_psum"), sem("ht_hi"), sem("ht_lo")
        pj_act, pj_dve = sem("pj_act"), sem("pj_dve")
        rev_full = [sem("rev_full0"), sem("rev_full1")]
        bias_ready = sem("bias_ready")
        qk_done, logit_done, exp_done, prob_done = sem("qk_done"), sem("logit_done"), sem("exp_done"), sem("prob_done")
        pT_psum, pT_act, pT_dve = sem("pT_psum"), sem("pT_act"), sem("pT_dve")
        pv_done, o_hi, o_lo = sem("pv_done"), sem("o_hi"), sem("o_lo")
        hnh_done, hnl_done = sem("hnh_done"), sem("hnl_done")
        rt_hi, rt_lo = sem("rt_hi"), sem("rt_lo")
        logits_psum, gap_done, e_done, sel_ready = sem("logits_psum"), sem("gap_done"), sem("e_done"), sem("sel_ready")
        rank_psum, ids_ready = sem("rank_psum"), sem("ids_ready")
        pick_ready = sem("pick_ready")
        ga_psum, ga_act, ga_dve = sem("ga_psum"), sem("ga_act"), sem("ga_dve")
        selT_psum, selT_ready = sem("selT_psum"), sem("selT_ready")
        y_hi, y_lo, sc_psum, x_added = sem("y_hi"), sem("y_lo"), sem("sc_psum"), sem("x_added")
        out_ready, stored = sem("out_ready"), sem("stored")

        C_IDENT, C_GAINT, C_BUCKET, C_RELB, C_POOL, C_SCALE, C_BAND, C_CLASS, C_TRI, C_IOTA, C_ROUTER, C_GAIN3, C_GAIN4 = range(13)
        CONST = [
            (ident[:], c_ident), (gainT[:], gains_t), (bucket[:], c_bucket), (relb[:], rel_bias),
            (poolM[:], c_pool.rearrange("(t p) g s -> p t g s", p=P)), (scaleT[:], a_scale),
            (band[:], c_band.rearrange("(t p) s -> p t s", p=P)),
            (classes[:], c_class.rearrange("c p s -> p c s")), (tri[:], c_tri.rearrange("c p s -> p c s")),
            (iota[:], c_iota.partition_broadcast(P)), (router[:], m_router[0].rearrange("(k p) e -> p k e", p=P)),
            (gain[:, 0], norm_ffn[1].partition_broadcast(P)), (gain[:, 1], norm_final.partition_broadcast(P)),
        ]

        def ffn_tile(gate_up, down, t):
            if t < DOWN:
                j, part, kh = t // 4, t % 4 // 2, t % 2
                c = part * FF + j * 512
                return gate_up[kh * 512:kh * 512 + 512, c:c + 512]
            n, kh = divmod(t - DOWN, DT)
            return down[kh * 512:kh * 512 + 512, n * 512:n * 512 + 512]

        def tile_source(t):
            if t < T_GROUP:
                return a_w_in[0][t % 2 * 512:t % 2 * 512 + 512, t // 2 * 512:t // 2 * 512 + 512]
            if t < T_FFN:
                t -= T_OUT
                return a_w_out[0][t % 2 * 512:t % 2 * 512 + 512, t // 2 * 512:t // 2 * 512 + 512]
            if t < T_ATT:
                return ffn_tile(f_w_gate_up[0], f_w_down[0], t - T_FFN)
            if t < T_MOE:
                half, s = divmod(t - T_ATT, HALF_TILES)
                if s < 18:
                    c = s // 2 * 1024 + half * 512
                    return b_w_in[0][s % 2 * 512:s % 2 * 512 + 512, c:c + 512]
                return b_w_out[0][half * 512:half * 512 + 512, (s - 18) * 512:(s - 17) * 512]
            return ffn_tile(m_w_gate_up[0, 0], m_w_down[0, 0], t - T_MOE)

        def make_hi(act, t, item=0):
            act.wait_ge(raw_full[t % RAW], item * (16 * (FFN_TILES // RAW)) + 16 * (t // RAW + 1))
            if t >= CUT:
                act.wait_ge(tile_used, item * FFN_TILES + t - CUT + 1)
            nc.scalar.activation(whi[:, t % CUT], raw[:, t % RAW], ACT.Copy).then_inc(hi_done, 1)

        def make_lo(dve, t, item=0):
            dve.wait_ge(hi_done, item * FFN_TILES + t + 1)
            if t >= CUT:
                dve.wait_ge(tile_used, item * FFN_TILES + t - CUT + 1)
            nc.vector.tensor_tensor(wlo[:, t % CUT], raw[:, t % RAW], whi[:, t % CUT].bitcast(F32),
                                    ALU.subtract).then_inc(lo_done, 1)

        def wblk(t, b):
            s = t % CUT
            return whi[:, s, b * 512:b * 512 + 512], wlo[:, s, b * 512:b * 512 + 512]

        def mm3(pe, dst, a, b, start, stop):
            pe.matmul(dst, a[0], b[0], start=start, stop=False)
            pe.matmul(dst, a[1], b[0], start=False, stop=False)
            return pe.matmul(dst, a[0], b[1], start=False, stop=stop)

        def tok(h, l, kb, tb):
            return h[:, kb, tb * P:tb * P + P], l[:, kb, tb * P:tb * P + P]

        sets = (G, U, Y0, Y1), (T, X, S0, S1)
        block = ctx.enter_context(nc.Block())

        @block.sync
        def _(sp):
            for a in range(4):
                sp.dma_start(x[a % 2 * 64:a % 2 * 64 + 64, a // 2, :],
                             x_in[0].rearrange("(m a) d -> a m d", a=4)[a]).then_inc(x_in_done, 16)

            def load(t, item=0, src=None):
                if t >= RAW:
                    sp.wait_ge(lo_done, item * FFN_TILES + t - RAW + 1)
                if t == T_GROUP:
                    dst = raw[:, t % RAW].rearrange("p (b n) -> p b n", n=256)
                    src = a_w_group[0].rearrange("g (c p) n -> p (g c) n", p=P)
                else:
                    dst = raw[:, t % RAW].rearrange("p (k n) -> p k n", n=512)
                    src = (tile_source(t) if src is None else src).rearrange("(k p) n -> p k n", p=P)
                sp.dma_start(dst, src).then_inc(raw_full[t % RAW], 16)

            def load_rev(c):
                if c == 0:
                    sp.wait_ge(toep_out, 16)
                    sp.wait_ge(x_sum, 4)
                if c >= 2:
                    sp.wait_ge(bias_ready, 2 * (c - 1))
                for a in range(4):
                    src = bass.AP(toep_dram.tensor, 2 * c * 512 + a, [[4, 64], [512, 2], [1, S]])
                    sp.dma_start(biasrev[a % 2 * 64:a % 2 * 64 + 64, c % 2, a // 2], src).then_inc(rev_full[c % 2], 16)

            for t in range(T_MOE + CUT):
                load(t)
                for half in range(2):
                    t0 = T_ATT + half * HALF_TILES
                    if t == t0 + RAW + CUT:
                        load_rev(4 * half)
                        load_rev(4 * half + 1)
                    if t == t0 + HALF_TILES + CUT:
                        load_rev(4 * half + 2)
                        load_rev(4 * half + 3)
            load_rev(6)
            load_rev(7)

            def item_tiles(i, e, e_next):
                gu, dn = m_w_gate_up[0, bass.ds(e, 1)], m_w_down[0, bass.ds(e, 1)]
                gu, dn = gu.rearrange("o k n -> (o k) n"), dn.rearrange("o k n -> (o k) n")
                for t in range(CUT, FFN_TILES):
                    load(T_MOE + t, i, ffn_tile(gu, dn, t))
                gu = m_w_gate_up[0, bass.ds(e_next, 1)].rearrange("o k n -> (o k) n")
                for t in range(CUT):
                    load(T_MOE + FFN_TILES + t, i, ffn_tile(gu, dn, t))

            with sp.Fori(0, E - 1) as i:
                item_tiles(i, i, i + 1)
            sp.wait_ge(ids_ready, 1)
            n_items = sp.value_load(ids[0:1, 0:1], min_val=E, max_val=ITEMS)
            with sp.Fori(E - 1, ITEMS) as i:
                with sp.If(i < n_items):
                    e = sp.value_load(ids[0:1, bass.ds(i - (E - 2), 1)], min_val=0, max_val=E - 1)
                    e_next = sp.value_load(ids[0:1, bass.ds(i - (E - 3), 1)], min_val=0, max_val=E - 1)
                    item_tiles(i, e, e_next)
                with sp.Else():
                    sp.nop()

            for a in range(4):
                if a % 2 == 0:
                    sp.wait_ge(out_ready, a // 2 + 1)
                sp.dma_start(out[0].rearrange("(m a) d -> a m d", a=4)[a],
                             hn[a % 2 * 64:a % 2 * 64 + 64, a // 2, :]).then_inc(stored, 16)
            sp.wait_ge(stored, 64)

        @block.gpsimd
        def _(pool):
            pool.wait_ge(c_in[C_BAND], 16)
            pool.wait_ge(c_in[C_CLASS], 16)
            per_part = 2 * 2 * 2 * S
            for h in range(HEADS):
                c = h // 2
                if h % 2 == 0:
                    pool.wait_ge(rev_full[c % 2], 64 * (c // 2 + 1))
                if h >= 2:
                    pool.wait_ge(logit_done, h - 1)
                for qt in range(2):
                    base = ((c % 2 * 2 + qt) * 2 + h % 2) * S + S - 1
                    rev = lambda a0, na: bass.AP(biasrev[:].tensor, base - a0, [[per_part, P], [-1, na], [-4, 64]])
                    to = bias[:, h % 2, qt]
                    nc.gpsimd.tensor_tensor(to[:, 0:S].rearrange("p (a m) -> p a m", a=4), rev(0, 4),
                                            band[:, qt].rearrange("p (a m) -> p a m", a=4), ALU.add)
                    for g in range(2):
                        last = nc.gpsimd.tensor_tensor(
                            to[:, S + g * P:S + g * P + P].rearrange("p (a m) -> p a m", a=2), rev(2 * qt, 2),
                            classes[:, g].rearrange("p (a m) -> p a m", a=2), ALU.add)
                last.then_inc(bias_ready, 1)

        @block.tensor
        def _(pe):
            def tile_ready(t, item=0):
                pe.wait_ge(lo_done, item * FFN_TILES + t + 1)

            def turn_x(n, kh):
                if n == 0:
                    pe.wait_ge(x_in_done, 64)
                else:
                    pe.wait_ge(x_sum, (2, 4, 8)[n - 1] - 1 + kh)
                for b, bank in ((0, G), (1, U)) if kh == 0 else ((2, T), (3, X)):
                    for kk in range(2):
                        for tb in range(NT):
                            mm = pe.transpose(bank[:, kk * S + tb * P:kk * S + tb * P + P],
                                              x[:, tb, (2 * b + kk) * P:(2 * b + kk + 1) * P], ident[:])
                    mm.then_inc(tx_psum, 1)

            def dense(t0, xh, xl, kbs, banks, after=()):
                done = 0
                for n, ks in enumerate(kbs):
                    tile_ready(t0 + n)
                    for tb in range(NT):
                        for b, kb in enumerate(ks):
                            mm = mm3(pe, banks[tb][:], tok(xh, xl, kb, tb), wblk(t0 + n, b),
                                     start=done + b == 0, stop=n == len(kbs) - 1 and b == len(ks) - 1)
                    done += len(ks)
                    mm.then_inc(tile_used, 1)
                    if n < len(after):
                        after[n]()

            def second_half(n):
                def turn():
                    turn_x(n, 1)
                    pe.wait_ge(tx_lo, 4 * n + 4)
                return turn

            KH = [range(0, 4), range(4, 8)]

            pe.wait_ge(c_in[C_IDENT], 16)
            turn_x(0, 0)
            turn_x(0, 1)
            pe.wait_ge(c_in[C_BUCKET], 16)
            pe.wait_ge(c_in[C_RELB], 16)
            pe.matmul(S0[0:HEADS, :], relb[:], bucket[:], start=True, stop=True).then_inc(toep_psum, 1)
            pe.wait_ge(tx_lo, 4)
            for n in range(2):
                dense(T_IN + 2 * n, xTh, xTl, KH, ((G, U), (Y0, Y1))[n])
            pe.wait_ge(u_act, 2)
            pe.wait_ge(u_dve, 2)
            pe.wait_ge(c_in[C_POOL], 16)
            pe.wait_ge(toep_sb, 1)
            for b, bank in enumerate((T, X, S0, S1)):
                for kk in range(2):
                    cb = 2 * b + kk
                    for tb in range(NT):
                        mm = pe.matmul(bank[:, kk * S:kk * S + S], u[:, tb, cb * P:cb * P + P],
                                       poolM[:, tb, cb // 2, :], start=tb == 0, stop=tb == NT - 1)
                mm.then_inc(mix_psum, 1)
            tile_ready(T_GROUP)
            for g, bank in enumerate((G, U, Y0, Y1)):
                pe.wait_ge(mix_lo, g + 1)
                for db in range(2):
                    for cb in range(2):
                        c = g * 512 + cb * S + db * P
                        w = whi[:, T_GROUP % CUT, c:c + P], wlo[:, T_GROUP % CUT, c:c + P]
                        r = mixTh[:, 2 * g + cb, :], mixTl[:, 2 * g + cb, :]
                        mm = mm3(pe, bank[:, db * S:db * S + S], w, r, start=cb == 0, stop=cb == 1)
                mm.then_inc(*((tile_used, 1) if g == 3 else (grp_psum, 1)))
            pe.wait_ge(grp_lo, 2)
            dense(T_OUT, yTh, yTl, KH, (T, X), [lambda: pe.wait_ge(grp_lo, 4)])
            dense(T_OUT + 2, yTh, yTl, KH, (Y0, Y1), [lambda: turn_x(1, 0)])

            pe.wait_ge(tx_lo, 6)

            def turn_hidden(j, width, src, ready):
                pe.wait_ge(h_ready, ready)
                for tb in range(width):
                    for c in range(4):
                        mm = pe.transpose((T, X)[tb][:, c * P:c * P + P], src(tb)[:, c * P:c * P + P], ident[:])
                    mm.then_inc(ht_psum, 1)

            for j in range(SLABS):
                t = T_FFN + 4 * j
                if j >= 1:
                    pe.wait_ge(silu_done, NT * j)
                dense(t, xTh, xTl, KH, (G, S0), [second_half(1)] if j == 0 else ())
                if j >= 1:
                    if j >= 2:
                        pe.wait_ge(ht_lo, NT * (j - 1))
                    turn_hidden(j - 1, NT, lambda tb: dh[:, tb], NT * j)
                dense(t + 2, xTh, xTl, KH, (U, S1))
            down = [range(4 * qn, 4 * qn + 4) for qn in range(DT)]
            acc = (Y0, Y1), (S0, S1)
            for n in range(2):
                for qn, ks in enumerate(down):
                    t = T_FFN + DOWN + DT * n + qn
                    if n == 0 and qn == 0:
                        pe.wait_ge(ht_lo, NT * (SLABS - 1))
                    if n == 0 and qn == 6:
                        pe.wait_ge(ht_lo, NT * SLABS)
                    tile_ready(t)
                    for tb in range(NT):
                        for b, kb in enumerate(ks):
                            mm = mm3(pe, acc[n][tb][:], (dTh[:, kb, tb], dTl[:, kb, tb]), wblk(t, b),
                                     start=kb == 0, stop=kb == KF - 1)
                    mm.then_inc(tile_used, 1)
                    if n == 0 and qn == 0:
                        turn_hidden(SLABS - 1, NT, lambda tb: dh[:, tb], NT * SLABS)
                    if n == 1 and qn == DT - 2:
                        turn_x(2, 0)

            pe.wait_ge(tx_lo, 10)

            def slab_read(n):
                if n % 3 == 2:
                    pe.wait_ge(pj_act, n // 3 + 1)
                else:
                    pe.wait_ge(pj_dve, n - n // 3 + 1)

            for half in range(2):
                t0 = T_ATT + half * HALF_TILES
                for s in range(9):
                    n = half * 9 + s
                    banks = sets[s % 2]
                    if s >= 2:
                        slab_read(n - 2)
                    if half == 1 and s == 1:
                        pe.wait_ge(x_sum, 6)
                    if s % 3 == 2:
                        dense(t0 + 2 * s, xTh, xTl, KH, banks)
                        continue
                    for kh in range(2):
                        tile_ready(t0 + 2 * s + kh)
                        for cb in range(4):
                            for b in range(4):
                                kb = 4 * kh + b
                                h_, l_ = wblk(t0 + 2 * s + kh, b)
                                mm = mm3(pe, banks[cb][:, 0:S], (h_[:, cb * P:cb * P + P], l_[:, cb * P:cb * P + P]),
                                         (xTh[:, kb], xTl[:, kb]), start=kb == 0, stop=kb == KD - 1)
                        mm.then_inc(tile_used, 1)
                        if n == 0 and kh == 0:
                            second_half(2)()
                    if n == 0:
                        pe.wait_ge(rdiag_done, 1)
                        for tb in range(NT):
                            mm = pe.matmul(S1[:, tb * P:tb * P + P], tri[:, 1], rdiag[:, tb], start=True, stop=True)
                        mm.then_inc(rcols_psum, 1)
                        pe.wait_ge(rcols_done, 1)

                def scores(h):
                    head = half * HH + h
                    r = h % 2 * HD
                    if h == 0:
                        slab_read(9 * half + 7)
                        slab_read(9 * half + 8)
                    if h >= 2:
                        pe.wait_ge(logit_done, head - 1)
                    for qt in range(2):
                        bank = ((G, U), (Y0, Y1))[h % 2][qt]
                        for g in range(3):
                            cols = slice(0, S) if g == 0 else slice(qt * P, qt * P + P)
                            to = slice(0, S) if g == 0 else slice(S + (g - 1) * P, S + g * P)
                            mm = pe.matmul(bank[:, to], q[r:r + HD, g, h // 2, qt * P:qt * P + P],
                                           k[r:r + HD, g, h // 2, cols], start=True, stop=True)
                    mm.then_inc(qk_done, 1)

                scores(0)
                scores(1)
                for h in range(HH):
                    head = half * HH + h
                    pe.wait_ge(prob_done, head + 1)
                    for qt in range(2):
                        for c in range(4):
                            mm = pe.transpose((T, X)[qt][:, c * P:c * P + P], logit[:, h % 2, qt, c * P:c * P + P], ident[:])
                    mm.then_inc(pT_psum, 1)
                    if h + 2 < HH:
                        scores(h + 2)
                    o = (S0, S1)[h // 2 % 2]
                    r = h % 2 * HD
                    pe.wait_ge(pT_act, head + 1)
                    pe.wait_ge(pT_dve, head + 1)
                    if h % 2 == 0 and head >= 4:
                        pe.wait_ge(o_lo, head // 2 - 1)
                    for kt in range(NT):
                        pe.matmul(o[r:r + HD, 0:S].rearrange("p (a b) -> p a b", a=2), v[:, kt, 0, h * HD:h * HD + HD],
                                  probsT[:, :, kt * P:kt * P + P], start=kt == 0, stop=False, skip_group_check=True)
                    for qt in range(2):
                        for g in (1, 2):
                            mm = pe.matmul(o[r:r + HD, qt * P:qt * P + P], v[:, qt, g, h * HD:h * HD + HD],
                                           probsT[:, qt, S + (g - 1) * P:S + g * P], start=False,
                                           stop=g == 2, skip_group_check=True)
                    mm.then_inc(pv_done, 1)
                pe.wait_ge(o_lo, 4 * half + 4)
                for n in range(2):
                    dense(t0 + 18 + n, oTh, oTl, [range(0, 4)], ((T, X), (S0, S1))[n])

            turn_x(3, 0)
            turn_x(3, 1)
            pe.wait_ge(rt_lo, 1)
            pe.wait_ge(tx_lo, 16)
            for tb in range(NT):
                for kb in range(KD):
                    mm = mm3(pe, Y0[:, tb * E:tb * E + E], tok(xTh, xTl, kb, tb), (routh[:, kb], routl[:, kb]),
                             start=kb == 0, stop=kb == KD - 1)
            mm.then_inc(logits_psum, 1)
            pe.wait_ge(c_in[C_TRI], 16)
            pe.wait_ge(sel_ready, 1)
            chosen = tiny[:, 4, :]
            pe.matmul(Y1[:, 0:E], tri[:, 0], chosen[:, 0:E], start=True, stop=True)
            pe.matmul(Y1[:, E:2 * E], tri[:, 1], chosen[:, 0:E], start=True, stop=False)
            pe.matmul(Y1[:, E:2 * E], tri[:, 0], chosen[:, E:2 * E], start=False, stop=True)
            pe.matmul(Y1[:, 2 * E:3 * E], tri[:, 1], chosen[:, 0:E], start=True, stop=False)
            pe.matmul(Y1[:, 2 * E:3 * E], tri[:, 1], chosen[:, E:2 * E], start=False, stop=True).then_inc(rank_psum, 1)

            def gather(n, rounds):
                for r in rounds:
                    bank, src = (G, U, T, X)[r], (hnh, hnl)[r // 2]
                    for kk in range(4):
                        kb = r % 2 * 4 + kk
                        for tb in range(NT):
                            mm = pe.matmul(bank[:, kk * P:kk * P + P], src[:, tb, kb * P:kb * P + P], sel[:, tb, :],
                                           start=tb == 0, stop=tb == NT - 1)
                    mm.then_inc(ga_psum, 1)

            pe.wait_ge(hnl_done, 2)
            pe.wait_ge(pick_ready, 1)
            gather(0, range(4))
            pe.wait_ge(ids_ready, 1)
            n_items = pe.value_load(ids[0:1, 0:1], min_val=E, max_val=ITEMS)

            def spread(n, count):
                pe.wait_ge(y_lo, count + 1)
                pe.wait_ge(x_added, count + 1)
                for tb in range(NT):
                    bank = (S0, S1)[tb]
                    pe.matmul(bank[:], selT[:, tb], yh[:, n * 512:n * 512 + 512], start=True, stop=False)
                    mm = pe.matmul(bank[:], selT[:, tb], yl[:, n * 512:n * 512 + 512], start=False, stop=True)
                mm.then_inc(sc_psum, 1)

            def item_body(i):
                pe.wait_ge(ga_act, i * 2 + 2)
                pe.wait_ge(ga_dve, i * 2 + 2)

                def product(t, xh, xl, ks, bank, last):
                    tile_ready(T_MOE + t, i)
                    for b, kb in enumerate(ks):
                        mm = mm3(pe, bank[:], (xh[:, kb], xl[:, kb]), wblk(T_MOE + t, b), start=kb == 0,
                                 stop=last and b == len(ks) - 1)
                    mm.then_inc(tile_used, 1)

                for j in range(SLABS):
                    if j >= 1:
                        pe.wait_ge(silu_done, i * SLABS + PAIRS0 + j)
                    product(4 * j, eTh, eTl, KH[0], G, False)
                    product(4 * j + 1, eTh, eTl, KH[1], G, True)
                    if j == 0:
                        spread(1, i * 2)
                    if j >= 1:
                        pe.wait_ge(ht_lo, i * SLABS + PAIRS0 + j - 1)
                        turn_hidden(j - 1, 1, lambda tb: mh[:], i * SLABS + PAIRS0 + j)
                    if j == 1:
                        for tb in range(NT):
                            mm = pe.transpose(X[:, tb * P:tb * P + P], sel[:, tb, :].bitcast(F32), ident[:])
                        mm.then_inc(selT_psum, 1)
                    product(4 * j + 2, eTh, eTl, KH[0], U, False)
                    product(4 * j + 3, eTh, eTl, KH[1], U, True)
                for n in range(2):
                    for qn, ks in enumerate(down):
                        if n == 0 and qn == 0:
                            pe.wait_ge(ht_lo, i * SLABS + PAIRS0 + SLABS - 1)
                        if n == 0 and qn == DT - 1:
                            pe.wait_ge(ht_lo, i * SLABS + PAIRS0 + SLABS)
                        product(DOWN + DT * n + qn, hTh, hTl, ks, (Y0, Y1)[n], qn == DT - 1)
                        if n == 0 and qn == 0:
                            turn_hidden(SLABS - 1, 1, lambda tb: mh[:], i * SLABS + PAIRS0 + SLABS)
                        if n == 1 and qn == 1:
                            pe.wait_ge(selT_ready, i + 1)
                            spread(0, i * 2 + 1)
                        if n == 1 and qn == 2:
                            pe.wait_ge(pick_ready, i + 2)
                            gather(i + 1, (0, 1))
                        if n == 1 and qn == 3:
                            gather(i + 1, (2, 3))

            with pe.Fori(0, ITEMS) as i:
                with pe.If(i < n_items):
                    item_body(i)
                with pe.Else():
                    pe.nop()
            spread(1, n_items * 2)

        @block.scalar
        def _(act):
            def load_const(ns):
                for n in ns:
                    act.dma_start(*CONST[n]).then_inc(c_in[n], 16)

            def copy(dst, src, s, scale=1.0):
                return nc.scalar.activation(dst, src, ACT.Copy, scale=scale).then_inc(s, 1)

            def root(n):
                act.wait_ge(ms_done, n + 1)
                nc.scalar.activation(std, ms, ACT.Sqrt).then_inc(std_done, 1)

            def cut_x(n, kh):
                for b, bank in ((0, G), (1, U)) if kh == 0 else ((2, T), (3, X)):
                    act.wait_ge(tx_psum, 4 * n + b + 1)
                    for kk in range(2):
                        kb = 2 * b + kk
                        last = nc.scalar.activation(xTh[:, kb], bank[:, kk * S:kk * S + S], ACT.Copy,
                                                    scale=gainT[:, n, kb:kb + 1])
                    last.then_inc(tx_hi, 1)

            def ahead(t):
                make_hi(act, t + CUT)

            load_const((C_IDENT, C_GAINT))
            act.wait_ge(c_in[C_GAINT], 16)
            cut_x(0, 0)
            cut_x(0, 1)
            load_const((C_BUCKET, C_RELB, C_SCALE))
            for t in range(CUT):
                make_hi(act, t)
            load_const((C_POOL,))
            root(0)
            act.wait_ge(toep_psum, 1)
            copy(toep[:], S0[0:HEADS, :], toep_sb, scale=-1.0)
            act.wait_ge(rstd_done, 1)
            for n in range(2):
                ahead(2 * n)
                act.wait_ge(tile_used, 2 * n + 2)
                copy(u[:, 0, n * 512:n * 512 + 512], ((G, Y0)[n])[:], u_act, scale=rstd[:, 0:1])
                ahead(2 * n + 1)
            for b, bank in enumerate((T, X, S0, S1)):
                act.wait_ge(mix_psum, b + 1)
                copy(mixTh[:, 2 * b:2 * b + 2, :].rearrange("p k s -> p (k s)"), bank[:], mix_hi)
            act.wait_ge(toep_sb, 1)
            act.dma_start(toep_dram, toep[:]).then_inc(toep_out, 16)
            act.wait_ge(c_in[C_SCALE], 16)
            for g, bank in enumerate((G, U, Y0, Y1)):
                if g < 3:
                    act.wait_ge(grp_psum, g + 1)
                else:
                    act.wait_ge(tile_used, T_GROUP + 1)
                for db in range(2):
                    last = nc.scalar.activation(yTh[:, 2 * g + db, :], bank[:, db * S:db * S + S], ACT.Copy,
                                                scale=scaleT[:, 2 * g + db:2 * g + db + 1])
                last.then_inc(grp_hi, 1)
            load_const((C_BAND, C_CLASS, C_TRI, C_IOTA, C_ROUTER, C_GAIN3, C_GAIN4))
            for t in range(T_GROUP, T_OUT + 3):
                ahead(t)
            cut_x(1, 0)
            ahead(T_OUT + 3)

            cut_x(1, 1)
            root(1)
            act.wait_ge(toep_out, 16)
            act.wait_ge(rstd_done, 2)
            for j in range(SLABS):
                t = T_FFN + 4 * j
                ahead(t)
                for tb in range(NT):
                    act.wait_ge(tile_used, t + 2)
                    if j >= 1:
                        act.wait_ge(h_ready, NT * j)
                    nc.scalar.activation(dsilu[:, tb], (G, S0)[tb][:], ACT.Silu, scale=rstd[:, tb:tb + 1]
                                         ).then_inc(silu_done, 1)
                ahead(t + 1)
                if j >= 1:
                    for tb in range(NT):
                        act.wait_ge(ht_psum, NT * (j - 1) + tb + 1)
                        copy(dTh[:, 4 * j - 4:4 * j, tb], (T, X)[tb][:].rearrange("p (c t) -> p c t", c=4), ht_hi)
                ahead(t + 2)
                ahead(t + 3)
            for t in range(DOWN, FFN_TILES):
                ahead(T_FFN + t)
                if t == DOWN:
                    for tb in range(NT):
                        act.wait_ge(ht_psum, NT * (SLABS - 1) + tb + 1)
                        copy(dTh[:, KF - 4:KF, tb], (T, X)[tb][:].rearrange("p (c t) -> p c t", c=4), ht_hi)
                if t == FFN_TILES - 2:
                    cut_x(2, 0)

            cut_x(2, 1)
            act.wait_ge(c_in[C_ROUTER], 16)
            copy(routh[:], router[:], rt_hi)
            root(2)
            act.wait_ge(rstd_done, 3)
            for half in range(2):
                t0 = T_ATT + half * HALF_TILES
                for s in range(9):
                    ahead(t0 + 2 * s)
                    ahead(t0 + 2 * s + 1)
                    if s % 3 == 2:
                        for tb in range(NT):
                            last = nc.scalar.activation(v[:, tb, s // 3], sets[s % 2][tb][:], ACT.Copy,
                                                        scale=rstd[:, tb:tb + 1])
                        last.then_inc(pj_act, 1)

                def exps(h):
                    act.wait_ge(logit_done, half * HH + h + 1)
                    for qt in range(2):
                        last = nc.scalar.activation(logit[:, h % 2, qt], logit[:, h % 2, qt], ACT.Exp, scale=-1.0,
                                                    bias=nmin[:, h % 2, qt:qt + 1], accum_out=rsum[:, h % 2, qt:qt + 1])
                    last.then_inc(exp_done, 1)

                def cut_o(pair):
                    act.wait_ge(pv_done, half * HH + 2 * pair + 2)
                    copy(oTh[:, pair], (S0, S1)[pair % 2][:, 0:S], o_hi)

                exps(0)
                for h in range(HH):
                    head = half * HH + h
                    if h + 1 < HH:
                        exps(h + 1)
                    act.wait_ge(pT_psum, head + 1)
                    if head >= 1:
                        act.wait_ge(pv_done, head)
                    copy(probsT[:, 0], T[:], pT_act)
                    if h % 2 == 0 and h >= 2:
                        cut_o(h // 2 - 1)
                cut_o(HH // 2 - 1)
                for n in range(2):
                    ahead(t0 + 18 + n)

            cut_x(3, 0)
            cut_x(3, 1)
            root(3)
            act.wait_ge(gap_done, 1)
            nc.scalar.activation(tiny[:, 1, 0:2], tiny[:, 0, 0:2], ACT.Exp).then_inc(e_done, 1)
            for tb in range(NT):
                act.wait_ge(hn_done, tb + 1)
                copy(hnh[:, tb], hn[:, tb], hnh_done)

            def cut_tokens(n):
                for r, bank in enumerate((G, U)):
                    act.wait_ge(ga_psum, 4 * n + r + 1)
                    copy(eTh[:, 4 * r:4 * r + 4].rearrange("p k t -> p (k t)"), bank[:], ga_act)

            cut_tokens(0)
            act.wait_ge(ids_ready, 1)
            n_items = act.value_load(ids[0:1, 0:1], min_val=E, max_val=ITEMS)

            def item_body(i):
                def ahead(t):
                    make_hi(act, T_MOE + t + CUT, i)

                def hidden_hi(j):
                    act.wait_ge(ht_psum, i * SLABS + PAIRS0 + j + 1)
                    copy(hTh[:, 4 * j:4 * j + 4].rearrange("p c t -> p (c t)"), T[:], ht_hi)

                def y_cut(n):
                    act.wait_ge(tile_used, i * FFN_TILES + T_MOE + DOWN + DT * n + DT)
                    copy(yh[:, n * 512:n * 512 + 512], (Y0, Y1)[n][:], y_hi)

                for j in range(SLABS):
                    ahead(4 * j)
                    act.wait_ge(tile_used, i * FFN_TILES + T_MOE + 4 * j + 2)
                    act.wait_ge(h_ready, i * SLABS + PAIRS0 + j)
                    nc.scalar.activation(msilu[:], G[:], ACT.Silu).then_inc(silu_done, 1)
                    ahead(4 * j + 1)
                    if j >= 1:
                        hidden_hi(j - 1)
                    ahead(4 * j + 2)
                    if j == 1:
                        act.wait_ge(selT_psum, i + 1)
                        copy(selT[:].rearrange("p t s -> p (t s)"), X[:, 0:S], selT_ready)
                    ahead(4 * j + 3)
                for t in range(DOWN, FFN_TILES):
                    ahead(t)
                    if t == DOWN:
                        hidden_hi(SLABS - 1)
                    if t == DOWN + DT - 1:
                        y_cut(0)
                    if t == DOWN + DT + 3:
                        cut_tokens(i + 1)
                y_cut(1)

            with act.Fori(0, ITEMS) as i:
                with act.If(i < n_items):
                    item_body(i)
                with act.Else():
                    act.nop()
            root(4)

        @block.vector
        def _(dve):
            links, sums = [0], [0]

            def link(ins):
                links[0] += 1
                ins.then_inc(chain, 1)
                dve.wait_ge(chain, links[0])

            def stats(n):
                for tb in range(NT):
                    last = nc.vector.tensor_tensor_reduce(hn[:, tb], x[:, tb], x[:, tb], 1.0, 0.0, ALU.mult, ALU.add,
                                                          accum_out=ss[:, tb:tb + 1])
                link(last)
                nc.vector.tensor_scalar(ms, ss, 1.0 / D, EPS, ALU.mult, ALU.add).then_inc(ms_done, 1)
                dve.wait_ge(std_done, n + 1)
                nc.vector.reciprocal(rstd, std).then_inc(rstd_done, 1)
                dve.wait_ge(rstd_done, n + 1)

            def norm(g, done):
                for tb in range(NT):
                    nc.vector.scalar_tensor_tensor(hn[:, tb], x[:, tb], rstd[:, tb:tb + 1], gain[:, g], ALU.mult,
                                                   ALU.mult).then_inc(done, 1)

            def lo(dst, src, hi, s):
                return nc.vector.tensor_tensor(dst, src, hi.bitcast(F32), ALU.subtract).then_inc(s, 1)

            def cut_x(n, kh):
                for b, bank in ((0, G), (1, U)) if kh == 0 else ((2, T), (3, X)):
                    dve.wait_ge(tx_hi, 4 * n + b + 1)
                    for kk in range(2):
                        kb = 2 * b + kk
                        last = nc.vector.scalar_tensor_tensor(xTl[:, kb], bank[:, kk * S:kk * S + S], gainT[:, n, kb:kb + 1],
                                                              xTh[:, kb].bitcast(F32), ALU.mult, ALU.subtract)
                    last.then_inc(tx_lo, 1)

            def ahead(t):
                make_lo(dve, t + CUT)

            def add_x(n, banks):
                for tb in range(NT):
                    sl = x[:, tb, n * 512:n * 512 + 512]
                    last = nc.vector.tensor_tensor(sl, banks[tb][:], sl, ALU.add)
                last.then_inc(x_sum, 1)
                sums[0] += 1
                dve.wait_ge(x_sum, sums[0])

            cut_x(0, 0)
            cut_x(0, 1)
            for t in range(CUT):
                make_lo(dve, t)
            dve.wait_ge(x_in_done, 64)
            stats(0)
            for n in range(2):
                ahead(2 * n)
                dve.wait_ge(tile_used, 2 * n + 2)
                nc.vector.tensor_scalar(u[:, 1, n * 512:n * 512 + 512], ((U, Y1)[n])[:], rstd[:, 1:2], None,
                                        ALU.mult).then_inc(u_dve, 1)
                ahead(2 * n + 1)
            for b, bank in enumerate((T, X, S0, S1)):
                dve.wait_ge(mix_hi, b + 1)
                f = lambda t: t[:, 2 * b:2 * b + 2, :].rearrange("p k s -> p (k s)")
                lo(f(mixTl), bank[:], f(mixTh), mix_lo)
            for g, bank in enumerate((G, U, Y0, Y1)):
                dve.wait_ge(grp_hi, g + 1)
                for db in range(2):
                    last = nc.vector.scalar_tensor_tensor(
                        yTl[:, 2 * g + db], bank[:, db * S:db * S + S], scaleT[:, 2 * g + db:2 * g + db + 1],
                        yTh[:, 2 * g + db].bitcast(F32), ALU.mult, ALU.subtract)
                last.then_inc(grp_lo, 1)
            for t in range(T_GROUP, T_OUT + 2):
                ahead(t)
            add_x(0, (T, X))
            ahead(T_OUT + 2)
            cut_x(1, 0)
            ahead(T_OUT + 3)
            add_x(1, (Y0, Y1))

            cut_x(1, 1)
            stats(1)
            for j in range(SLABS):
                t = T_FFN + 4 * j
                ahead(t)
                ahead(t + 1)
                if j >= 1:
                    for tb in range(NT):
                        dve.wait_ge(ht_hi, NT * (j - 1) + tb + 1)
                        lo(dTl[:, 4 * j - 4:4 * j, tb], (T, X)[tb][:].rearrange("p (c t) -> p c t", c=4),
                           dTh[:, 4 * j - 4:4 * j, tb], ht_lo)
                ahead(t + 2)
                dve.wait_ge(tile_used, t + 4)
                for tb in range(NT):
                    dve.wait_ge(silu_done, NT * j + tb + 1)
                    if j >= 1:
                        dve.wait_ge(ht_psum, NT * j)
                    nc.vector.scalar_tensor_tensor(dh[:, tb], (U, S1)[tb][:], rstd[:, tb:tb + 1], dsilu[:, tb],
                                                   ALU.mult, ALU.mult).then_inc(h_ready, 1)
                ahead(t + 3)
            for t in range(DOWN, FFN_TILES):
                ahead(T_FFN + t)
                if t == DOWN:
                    for tb in range(NT):
                        dve.wait_ge(ht_hi, NT * (SLABS - 1) + tb + 1)
                        lo(dTl[:, KF - 4:KF, tb], (T, X)[tb][:].rearrange("p (c t) -> p c t", c=4),
                           dTh[:, KF - 4:KF, tb], ht_lo)
                if t == DOWN + DT - 1:
                    add_x(0, (Y0, Y1))
                if t == FFN_TILES - 2:
                    cut_x(2, 0)
            add_x(1, (S0, S1))

            cut_x(2, 1)
            stats(2)
            for tb in range(NT):
                last = nc.vector.tensor_scalar(rdiag[:, tb], ident[:], rstd[:, tb:tb + 1], None, ALU.mult)
            last.then_inc(rdiag_done, 1)
            dve.wait_ge(rt_hi, 1)
            lo(routl[:], router[:], routh[:], rt_lo)
            for half in range(2):
                t0 = T_ATT + half * HALF_TILES
                for s in range(9):
                    g, kind = divmod(s, 3)
                    ahead(t0 + 2 * s)
                    ahead(t0 + 2 * s + 1)
                    if half == 0 and s == 0:
                        dve.wait_ge(rcols_psum, 1)
                        nc.vector.tensor_copy(rcols[:], S1[:, 0:S]).then_inc(rcols_done, 1)
                        dve.wait_ge(rcols_done, 1)
                    if kind < 2:
                        for cb in range(4):
                            last = nc.vector.scalar_tensor_tensor((q, k)[kind][:, g, cb], sets[s % 2][cb][:, 0:S],
                                                                  (-0.125, 1.0)[kind], rcols[:], ALU.mult, ALU.mult)
                        last.then_inc(pj_dve, 1)

                def logits(h):
                    head = half * HH + h
                    dve.wait_ge(qk_done, head + 1)
                    dve.wait_ge(bias_ready, head + 1)
                    for qt in range(2):
                        last = nc.vector.tensor_tensor_reduce(
                            logit[:, h % 2, qt], ((G, U), (Y0, Y1))[h % 2][qt][:], bias[:, h % 2, qt], 1.0, 3.0e38,
                            ALU.add, ALU.min, accum_out=nmin[:, h % 2, qt:qt + 1])
                    last.then_inc(logit_done, 1)

                def cut_o(pair):
                    dve.wait_ge(o_hi, half * 4 + pair + 1)
                    lo(oTl[:, pair], (S0, S1)[pair % 2][:, 0:S], oTh[:, pair], o_lo)

                logits(0)
                logits(1)
                for h in range(HH):
                    head = half * HH + h
                    dve.wait_ge(exp_done, head + 1)
                    link(nc.vector.reciprocal(rinv[:, h % 2], rsum[:, h % 2]))
                    for qt in range(2):
                        last = nc.vector.tensor_scalar(logit[:, h % 2, qt], logit[:, h % 2, qt],
                                                       rinv[:, h % 2, qt:qt + 1], None, ALU.mult)
                    last.then_inc(prob_done, 1)
                    dve.wait_ge(pT_psum, head + 1)
                    if head >= 1:
                        dve.wait_ge(pv_done, head)
                    nc.vector.tensor_copy(probsT[:, 1], X[:]).then_inc(pT_dve, 1)
                    if h + 2 < HH:
                        logits(h + 2)
                    if h % 2 == 0 and h >= 2:
                        cut_o(h // 2 - 1)
                cut_o(HH // 2 - 1)
                for n in range(2):
                    ahead(t0 + 18 + n)
                    add_x(n, ((T, X), (S0, S1))[n])

            cut_x(3, 0)
            cut_x(3, 1)
            stats(3)
            gap, ex, gates, chosen, picked, gatev = (tiny[:, i, :] for i in (0, 1, 2, 4, 5, 6))
            logs, best, idxf = tiny[:, 7, :], tiny[:, 8, :], tiny[:, 9, 0:4]
            place_, over_place, full, kth, mask = (tiny[:, i, :] for i in (10, 11, 12, 13, 14))
            junk, eid = tiny[:, 15, 0:8], tiny[:, 3, :]
            two = lambda t: t.rearrange("p (t e) -> p t e", e=E)
            dve.wait_ge(logits_psum, 1)
            for tb in range(NT):
                last = nc.vector.tensor_scalar(logs[:, tb * 8:tb * 8 + 8], Y0[:, tb * 8:tb * 8 + 8], rstd[:, tb:tb + 1], None,
                                               ALU.mult)
            link(last)
            for tb in range(NT):
                link(nc.vector.max(best[:, tb * 8:tb * 8 + 8], logs[:, tb * 8:tb * 8 + 8]))
            nc.vector.tensor_tensor(gap[:, 0:2], two(best)[:, :, 1], two(best)[:, :, 0], ALU.subtract).then_inc(gap_done, 1)
            for tb in range(NT):
                link(nc.vector.max_index(idx[:, tb], best[:, tb * 8:tb * 8 + 8], logs[:, tb * 8:tb * 8 + 8]))
            link(nc.vector.tensor_copy(idxf.rearrange("p (t c) -> p t c", c=2), idx[:, :, 0:2]))
            dve.wait_ge(c_in[C_IOTA], 16)
            first, second = picked, gatev
            for tb in range(NT):
                sl = slice(tb * 8, tb * 8 + 8)
                nc.vector.tensor_scalar(first[:, sl], iota[:, P:P + 8], idxf[:, 2 * tb:2 * tb + 1], None, ALU.is_equal)
                last = nc.vector.tensor_scalar(second[:, sl], iota[:, P:P + 8], idxf[:, 2 * tb + 1:2 * tb + 2], None, ALU.is_equal)
            link(last)
            nc.vector.tensor_tensor(chosen, first, second, ALU.add).then_inc(sel_ready, 1)
            dve.wait_ge(sel_ready, 1)
            dve.wait_ge(c_in[C_GAIN3], 16)
            norm(0, hn_done)
            dve.wait_ge(e_done, 1)
            link(nc.vector.tensor_scalar(gates[:, 0:2], ex[:, 0:2], 1.0, None, ALU.add))
            link(nc.vector.reciprocal(gates[:, 2:4], gates[:, 0:2]))
            link(nc.vector.tensor_tensor(gates[:, 4:6], ex[:, 0:2], gates[:, 2:4], ALU.mult))
            for tb in range(NT):
                sl = slice(tb * 8, tb * 8 + 8)
                link(nc.vector.tensor_scalar(junk, first[:, sl], gates[:, 2 + tb:3 + tb], None, ALU.mult))
                link(nc.vector.scalar_tensor_tensor(gate_item[:, tb, 1:E + 1], second[:, sl], gates[:, 4 + tb:5 + tb], junk,
                                                    ALU.mult, ALU.add))
            dve.wait_ge(rank_psum, 1)
            for tb in range(NT):
                sl = slice(tb * 8, tb * 8 + 8)
                nc.vector.scalar_tensor_tensor(rank_item[:, tb, 0:E], Y1[:, sl], SHIFT, chosen[:, sl], ALU.add, ALU.mult)
                last = nc.vector.scalar_tensor_tensor(over_place[:, sl], Y1[:, sl], SHIFT - CAP, chosen[:, sl],
                                                      ALU.add, ALU.mult)
            link(last)

            def pick(n):
                for tb in range(NT):
                    last = nc.vector.tensor_scalar(sel[:, tb], iota[:, 0:P], rank_item[:, tb, bass.ds(n, 1)], None, ALU.is_equal)
                last.then_inc(pick_ready, 1)


            pick(0)
            for tb in range(NT):
                dve.wait_ge(hnh_done, tb + 1)
                lo(hnl[:, tb], hn[:, tb], hnh[:, tb], hnl_done)
            nc.vector.memset(kth, 0.0)
            nc.vector.memset(full, 0.0)
            link(nc.vector.memset(mask, 0.0))
            link(nc.vector.tensor_scalar(full[:, 8:16], Y1[:, 16:24], float(CAP), None, ALU.is_gt))
            link(nc.vector.tensor_tensor(kth[:, 8:16], full[:, 8:16], full[:, 7:15], ALU.add))
            link(nc.vector.tensor_tensor(mask[:, 8:16], kth[:, 8:16], kth[:, 6:14], ALU.add))
            link(nc.vector.tensor_tensor(kth[:, 8:16], mask[:, 8:16], mask[:, 4:12], ALU.add))
            link(nc.vector.tensor_scalar(eid[:, 0:1], kth[:, 15:16], float(E), None, ALU.add))
            link(nc.vector.tensor_tensor(kth[:, 0:8], kth[:, 8:16], full[:, 8:16], ALU.mult))
            nc.vector.memset(eid[:, 2 + OVER:3 + OVER], 0.0)
            link(nc.vector.memset(eid[:, 1:2], float(E - 1)))
            for n in range(OVER):
                link(nc.vector.tensor_scalar(mask[:, 0:8], kth[:, 0:8], float(n + 1), None, ALU.is_equal))
                link(nc.vector.tensor_tensor_reduce(junk, mask[:, 0:8], iota[:, P:P + 8], 1.0, 0.0, ALU.mult, ALU.add,
                                                    accum_out=eid[:, 2 + n:3 + n]))
                for tb in range(NT):
                    sl = slice(tb * 8, tb * 8 + 8)
                    link(nc.vector.tensor_tensor_reduce(junk, mask[:, 0:8], over_place[:, sl], 1.0, 0.0, ALU.mult, ALU.add,
                                                        accum_out=rank_item[:, tb, E + n:E + n + 1]))
                    link(nc.vector.tensor_tensor_reduce(junk, mask[:, 0:8], gate_item[:, tb, 1:E + 1], 1.0, 0.0, ALU.mult, ALU.add,
                                                        accum_out=gate_item[:, tb, E + n + 1:E + n + 2]))
            nc.vector.memset(gate_item[:, :, 0:1], 0.0)
            nc.vector.memset(rank_item[:, :, ITEMS:ITEMS + 1], 0.0).then_inc(x_added, 1)
            nc.vector.memset(selT[:].bitcast(F32), 0.0)
            nc.vector.memset(yh[:].bitcast(F32), 0.0)
            nc.vector.memset(yl[:].bitcast(F32), 0.0).then_inc(y_lo, 1)
            nc.vector.tensor_copy(ids[:, 0:3 + OVER], eid[:, 0:3 + OVER]).then_inc(ids_ready, 1)

            def tokens_lo(n):
                for r, bank in enumerate((T, X)):
                    dve.wait_ge(ga_psum, 4 * n + r + 3)
                    nc.vector.tensor_copy(eTl[:, 4 * r:4 * r + 4].rearrange("p k t -> p (k t)"), bank[:]).then_inc(ga_dve, 1)

            tokens_lo(0)
            dve.wait_ge(ids_ready, 1)
            n_items = dve.value_load(ids[0:1, 0:1], min_val=E, max_val=ITEMS)

            def add_item(n, count, column):
                dve.wait_ge(sc_psum, count + 1)
                dve.wait_ge(x_added, count + 1)
                for tb in range(NT):
                    sl = x[:, tb, n * 512:n * 512 + 512]
                    last = nc.vector.scalar_tensor_tensor(sl, (S0, S1)[tb][:], gate_item[:, tb, bass.ds(column, 1)], sl,
                                                          ALU.mult, ALU.add)
                last.then_inc(x_added, 1)

            def item_body(i):
                def ahead(t):
                    make_lo(dve, T_MOE + t + CUT, i)

                def hidden_lo(j):
                    dve.wait_ge(ht_hi, i * SLABS + PAIRS0 + j + 1)
                    f = lambda t: t[:, 4 * j:4 * j + 4].rearrange("p c t -> p (c t)")
                    lo(f(hTl), T[:], f(hTh), ht_lo)

                def y_cut(n):
                    dve.wait_ge(y_hi, i * 2 + n + 1)
                    sl = slice(n * 512, n * 512 + 512)
                    lo(yl[:, sl], (Y0, Y1)[n][:], yh[:, sl], y_lo)

                for j in range(SLABS):
                    ahead(4 * j)
                    ahead(4 * j + 1)
                    if j == 0:
                        add_item(1, i * 2, i)
                    if j >= 1:
                        hidden_lo(j - 1)
                    if j == 2:
                        dve.wait_ge(selT_psum, i + 1)
                        pick(i + 1)
                    ahead(4 * j + 2)
                    dve.wait_ge(tile_used, i * FFN_TILES + T_MOE + 4 * j + 4)
                    dve.wait_ge(silu_done, i * SLABS + PAIRS0 + j + 1)
                    dve.wait_ge(ht_psum, i * SLABS + PAIRS0 + j)
                    nc.vector.tensor_tensor(mh[:], U[:], msilu[:], ALU.mult).then_inc(h_ready, 1)
                    ahead(4 * j + 3)
                for t in range(DOWN, FFN_TILES):
                    ahead(t)
                    if t == DOWN:
                        hidden_lo(SLABS - 1)
                    if t == DOWN + DT - 1:
                        y_cut(0)
                    if t == DOWN + DT + 2:
                        add_item(0, i * 2 + 1, i + 1)
                    if t == DOWN + DT + 4:
                        tokens_lo(i + 1)
                y_cut(1)

            with dve.Fori(0, ITEMS) as i:
                with dve.If(i < n_items):
                    item_body(i)
                with dve.Else():
                    dve.nop()
            add_item(1, n_items * 2, n_items)
            dve.wait_ge(x_added, n_items * 2 + 2)
            stats(4)
            dve.wait_ge(c_in[C_GAIN4], 16)
            norm(1, out_ready)


def constants():
    import numpy as np
    pos = np.array([4 * (p % 64) + p // 64 for p in range(S)])
    pool = np.zeros((S, 4, S), np.float32)
    for g, w in enumerate((2, 4, 8, 16)):
        lo = np.clip(pos - w // 2, 0, S)
        hi = np.clip(pos + w - w // 2, 0, S)
        inside = (pos[:, None] >= lo[None]) & (pos[:, None] < hi[None])
        pool[:, g] = inside / (hi - lo)[None].astype(np.float64) - (pos[:, None] == pos[None])
    rel = S - 1 - np.arange(512)
    n = np.abs(rel)
    big = 8 + (np.log(np.maximum(n, 1) / 8.0) / np.log(1024 / 8.0) * 8).astype(np.int32)
    b = np.where(rel > 0, 16, 0) + np.where(n < 8, n, np.minimum(big, 15))
    bucket = (np.arange(32)[:, None] == b[None]).astype(np.float32)
    d = pos[None] - pos[:, None]
    band = np.where(np.abs(d) <= 64, 0.0, BIG).astype(np.float32)
    same = d[:P, :P]
    classes = np.stack([np.where(same % m == 0, 0.0, BIG) for m in (4, 16)]).astype(np.float32)
    tri = np.stack([np.arange(P)[:, None] < np.arange(P)[None], np.ones((P, P))]).astype(np.float32)
    slots = np.where(np.arange(P) < CAP, np.arange(P) + SHIFT, -1.0)
    iota = np.concatenate([slots, np.arange(8)]).astype(np.float32)
    return {"ident": np.eye(P, dtype=np.float32), "pool": pool, "bucket": bucket, "band": band,
            "class": classes, "tri": tri, "iota": iota}


_INS = ["x", "rel_bias", "gains_t", "norm_ffn", "norm_final", "a_w_in", "a_w_group", "a_scale", "a_w_out",
        "b_w_in", "b_w_out", "f_w_gate_up", "f_w_down", "m_router", "m_w_gate_up", "m_w_down"]


def kernel(**inputs):
    import numpy as _np
    import concourse.bacc as _bacc
    from concourse import mybir as _mybir
    from concourse.bass_utils import run_bass_kernel_spmd as _run

    nc = _bacc.Bacc("TRN2", target_bir_lowering=False, num_devices=1, dynamic_dma_scratch_size=128)
    gains = [inputs["norm_mix"][0], inputs["norm_ffn"][0], inputs["norm_mix"][1], inputs["norm_ffn"][1]]
    inputs = dict(inputs, gains_t=_np.stack([_np.asarray(g).reshape(KD, P).T for g in gains], axis=1))
    data = {n: _np.ascontiguousarray(inputs[n]) for n in _INS}
    data["a_scale"] = _np.ascontiguousarray(data["a_scale"].reshape(KD, P).T)
    data.update({f"const_{n}": a for n, a in constants().items()})
    arrays, args = {}, []
    for name, a in data.items():
        arrays[f"in_{name}_dram"] = a
        args.append(nc.dram_tensor(f"in_{name}_dram", a.shape, _mybir.dt.from_np(a.dtype), kind="ExternalInput").ap())
    args.append(nc.dram_tensor("out_0_dram", (1, S, D), _mybir.dt.float32, kind="ExternalOutput").ap())
    encoder(nc, *args)
    r = _run(nc, [arrays], core_ids=[0])
    return r.results[0]["out_0_dram"]
```

```python
from contextlib import ExitStack

import concourse.bass as bass
from concourse import mybir

P = 128
RAW = 7
CUT = 3
D = 1024
S = 256
NT = S // P
KD = D // P
FF = 3584
KF = FF // P
SLABS = FF // 512
HD = 64
HEADS = 16
HH = HEADS // 2
E = 8
CAP = 128
OVER = (2 * S) // (CAP + 1)
ITEMS = E + OVER
EPS = 1e-6
SHIFT = 1000.0
BIG = 1.0e30

ALU = mybir.AluOpType
ACT = mybir.ActivationFunctionType
F32 = mybir.dt.float32
F32R = mybir.dt.float32r
I32 = mybir.dt.int32
U32 = mybir.dt.uint32

T_IN = 0
T_GROUP = 4
T_OUT = 5
T_FFN = 9
DOWN = 4 * SLABS
DT = KF // 4
FFN_TILES = DOWN + 2 * DT
T_ATT = T_FFN + FFN_TILES
HALF_TILES = 20
T_MOE = T_ATT + 2 * HALF_TILES
PAIRS0 = SLABS * NT


def encoder(nc, x_in, rel_bias, gains_t, norm_ffn, norm_final, a_w_in, a_w_group, a_scale, a_w_out,
            b_w_in, b_w_out, f_w_gate_up, f_w_down, m_router, m_w_gate_up, m_w_down,
            c_ident, c_pool, c_bucket, c_band, c_class, c_tri, c_iota, out):
    with ExitStack() as ctx:
        sem = lambda name: ctx.enter_context(nc.semaphore(name))
        psum = lambda name: ctx.enter_context(nc.psum_tensor(name, [P, 512], F32))

        arena_bytes = (nc.sbuf_usable_end - nc.sbuf_base - 64) // 64 * 64
        arena = ctx.enter_context(nc.sbuf_tensor("arena", [P, arena_bytes // 4], F32))
        top = [nc.sbuf_base - arena_bytes]
        limit = nc.sbuf_base

        def place(name, shape, dt, parts=P):
            n = 4
            for s in shape:
                n *= s
            t = nc.alloc_sbuf_tensor_at(name, [parts] + list(shape), dt, offset=top[0])
            top[0] += (n + 31) // 32 * 32
            assert top[0] <= limit, (name, top[0] - limit)
            return t

        raw = place("raw", [RAW, 2048], F32)
        whi = place("whi", [CUT, 2048], F32R)
        wlo = place("wlo", [CUT, 2048], F32R)
        x = place("x", [NT, D], F32)
        at_gain = top[0]
        gain = place("gain", [2, D], F32)
        end_gain, top[0] = top[0], at_gain
        biasrev = place("biasrev", [2, 2, 2, S], F32)
        assert top[0] <= end_gain
        top[0] = end_gain
        gainT = place("gainT", [4, KD], F32)
        xTh = place("xTh", [KD, S], F32R)
        xTl = place("xTl", [KD, S], F32R)
        ident = place("ident", [P], F32)
        band = place("band", [NT, S], F32)
        classes = place("classes", [2, P], F32)
        tri = place("tri", [2, P], F32)
        iota = place("iota", [P + 8], F32)
        scaleT = place("scaleT", [KD], F32)
        router = place("router", [KD, E], F32)
        routh = place("routh", [KD, E], F32R)
        routl = place("routl", [KD, E], F32R)
        rdiag = place("rdiag", [NT, P], F32)
        rcols = place("rcols", [S], F32)
        logitsT = rcols[0:E, :]
        small = place("small", [16], F32)
        ss, ms, std, rstd = (small[:, 2 * i:2 * i + 2] for i in range(4))
        nmin = place("nmin", [2, 2], F32)
        rsum = place("rsum", [2, 2], F32)
        rinv = place("rinv", [2, 2], F32)
        rank_item = place("rank_item", [NT, ITEMS + 1], F32)
        gate_item = place("gate_item", [NT, ITEMS + 1], F32)
        ids = place("ids", [16], I32)
        at_hn = top[0]
        hn = place("hn", [NT, D], F32)
        phase = top[0]
        top[0] = at_hn
        probsT = place("probsT", [2, 2, 512], F32)

        top[0] = phase
        poolM = place("poolM", [NT, 4, S], F32)
        u = place("u", [NT, D], F32)
        mixTh = place("mixTh", [KD, S], F32R)
        mixTl = place("mixTl", [KD, S], F32R)
        yTh = place("yTh", [KD, S], F32R)
        yTl = place("yTl", [KD, S], F32R)
        bucket = place("bucket", [512], F32, parts=32)
        relb = place("relb", [HEADS], F32, parts=32)
        toep = place("toep", [512], F32, parts=HEADS)

        top[0] = phase
        dTh = place("dTh", [KF, NT, P], F32R)
        dTl = place("dTl", [KF, NT, P], F32R)
        dsilu = place("dsilu", [NT, 512], F32)
        dh = place("dh", [NT, 512], F32)

        top[0] = phase
        q = place("q", [3, 4, S], F32)
        k = place("k", [3, 4, S], F32)
        v = place("v", [NT, 3, 512], F32)
        logit = place("logit", [2, 2, 512], F32)
        oTh = place("oTh", [4, S], F32R)
        oTl = place("oTl", [4, S], F32R)
        bias = place("bias", [4, 2, 512], F32)

        top[0] = phase
        hnh = place("hnh", [NT, D], F32R)
        hnl = place("hnl", [NT, D], F32R)
        eTh = place("eTh", [KD, P], F32R)
        eTl = place("eTl", [KD, P], F32R)
        at_h = top[0]
        squares = place("squares", [NT, D], F32)
        top[0] = at_h
        hTh = place("hTh", [KF, P], F32R)
        hTl = place("hTl", [KF, P], F32R)
        mbuf = place("mbuf", [2, 512], F32)
        msilu, mh = mbuf[:, 0], mbuf[:, 1]
        yh = place("yh", [D], F32R)
        yl = place("yl", [D], F32R)
        sel = place("sel", [NT, P], F32R)
        selT = place("selT", [NT, P], F32R)
        tiny = place("tiny", [16, 16], F32)
        scrap = place("scrap", [2 + 5 * OVER, E], F32)
        idx = place("idx", [NT, 8], U32)

        G, U, T, X, Y0, Y1, S0, S1 = (psum(n) for n in ("bG", "bU", "bT", "bX", "bY0", "bY1", "bS0", "bS1"))
        toep_dram = nc.dram_tensor("toeplitz", (HEADS, 512), F32, kind="Internal").ap()

        x_in_done = sem("x_in_done")
        c_in = [sem(f"const{i}") for i in range(13)]
        raw_full = [sem(f"raw_full{i}") for i in range(RAW)]
        hi_done, lo_done, tile_used = sem("hi_done"), sem("lo_done"), sem("tile_used")
        chain = sem("chain")
        ms_done, std_done, hn_done = sem("ms_done"), sem("std_done"), sem("hn_done")
        rstd_done, x_sum, sq_done = sem("rstd_done"), sem("x_sum"), sem("sq_done")
        rdiag_done, rcols_psum, rcols_done = sem("rdiag_done"), sem("rcols_psum"), sem("rcols_done")
        tx_psum, tx_hi, tx_lo = sem("tx_psum"), sem("tx_hi"), sem("tx_lo")
        u_act, u_dve = sem("u_act"), sem("u_dve")
        mix_psum, mix_hi, mix_lo = sem("mix_psum"), sem("mix_hi"), sem("mix_lo")
        grp_psum, grp_hi, grp_lo = sem("grp_psum"), sem("grp_hi"), sem("grp_lo")
        toep_psum, toep_sb, toep_out = sem("toep_psum"), sem("toep_sb"), sem("toep_out")
        silu_done, h_ready = sem("silu_done"), sem("h_ready")
        ht_psum, ht_hi, ht_lo = sem("ht_psum"), sem("ht_hi"), sem("ht_lo")
        pj_act, pj_dve = sem("pj_act"), sem("pj_dve")
        rev_full = [sem("rev_full0"), sem("rev_full1")]
        bias_ready = sem("bias_ready")
        qk_done, logit_done, exp_done, prob_done = sem("qk_done"), sem("logit_done"), sem("exp_done"), sem("prob_done")
        pT_psum, pT_sb = sem("pT_psum"), sem("pT_sb")
        pv_done, o_hi, o_lo = sem("pv_done"), sem("o_hi"), sem("o_lo")
        hnh_done, hnl_done = sem("hnh_done"), sem("hnl_done")
        rt_hi, rt_lo = sem("rt_hi"), sem("rt_lo")
        lt_psum, lt_sb = sem("lt_psum"), sem("lt_sb")
        logits_psum, gap_done, e_done, sel_ready = sem("logits_psum"), sem("gap_done"), sem("e_done"), sem("sel_ready")
        rank_psum, ids_ready = sem("rank_psum"), sem("ids_ready")
        pick_ready = sem("pick_ready")
        ga_psum, ga_sb = sem("ga_psum"), sem("ga_sb")
        selT_psum, selT_ready = sem("selT_psum"), sem("selT_ready")
        y_hi, y_lo, sc_psum, x_added = sem("y_hi"), sem("y_lo"), sem("sc_psum"), sem("x_added")
        x_final, out_ready, stored = sem("x_final"), [sem("out_ready0"), sem("out_ready1")], sem("stored")

        C_IDENT, C_GAINT, C_BUCKET, C_RELB, C_POOL, C_SCALE, C_BAND, C_CLASS, C_TRI, C_IOTA, C_ROUTER, C_GAIN3, C_GAIN4 = range(13)
        CONST = [
            (ident[:], c_ident), (gainT[:], gains_t), (bucket[:], c_bucket), (relb[:], rel_bias),
            (poolM[:], c_pool.rearrange("(t p) g s -> p t g s", p=P)), (scaleT[:], a_scale),
            (band[:], c_band.rearrange("(t p) s -> p t s", p=P)),
            (classes[:], c_class.rearrange("c p s -> p c s")), (tri[:], c_tri.rearrange("c p s -> p c s")),
            (iota[:], c_iota.partition_broadcast(P)), (router[:], m_router[0].rearrange("(k p) e -> p k e", p=P)),
            (gain[:, 0], norm_ffn[1].partition_broadcast(P)), (gain[:, 1], norm_final.partition_broadcast(P)),
        ]

        def ffn_tile(gate_up, down, t):
            if t < DOWN:
                j, part, kh = t // 4, t % 4 // 2, t % 2
                c = part * FF + j * 512
                return gate_up[kh * 512:kh * 512 + 512, c:c + 512]
            n, kh = divmod(t - DOWN, DT)
            return down[kh * 512:kh * 512 + 512, n * 512:n * 512 + 512]

        def tile_source(t):
            if t < T_GROUP:
                return a_w_in[0][t % 2 * 512:t % 2 * 512 + 512, t // 2 * 512:t // 2 * 512 + 512]
            if t < T_FFN:
                t -= T_OUT
                return a_w_out[0][t % 2 * 512:t % 2 * 512 + 512, t // 2 * 512:t // 2 * 512 + 512]
            if t < T_ATT:
                return ffn_tile(f_w_gate_up[0], f_w_down[0], t - T_FFN)
            if t < T_MOE:
                half, s = divmod(t - T_ATT, HALF_TILES)
                if s < 18:
                    c = s // 2 * 1024 + half * 512
                    return b_w_in[0][s % 2 * 512:s % 2 * 512 + 512, c:c + 512]
                return b_w_out[0][half * 512:half * 512 + 512, (s - 18) * 512:(s - 17) * 512]
            return ffn_tile(m_w_gate_up[0, 0], m_w_down[0, 0], t - T_MOE)

        def make_hi(act, t, item=0):
            act.wait_ge(raw_full[t % RAW], item * (16 * (FFN_TILES // RAW)) + 16 * (t // RAW + 1))
            if t >= CUT:
                act.wait_ge(tile_used, item * FFN_TILES + t - CUT + 1)
            nc.scalar.activation(whi[:, t % CUT], raw[:, t % RAW], ACT.Copy).then_inc(hi_done, 1)

        def make_lo(dve, t, item=0):
            dve.wait_ge(hi_done, item * FFN_TILES + t + 1)
            if t >= CUT:
                dve.wait_ge(tile_used, item * FFN_TILES + t - CUT + 1)
            nc.vector.tensor_tensor(wlo[:, t % CUT], raw[:, t % RAW], whi[:, t % CUT].bitcast(F32),
                                    ALU.subtract).then_inc(lo_done, 1)

        def wblk(t, b):
            s = t % CUT
            return whi[:, s, b * 512:b * 512 + 512], wlo[:, s, b * 512:b * 512 + 512]

        def mm3(pe, dst, a, b, start, stop):
            pe.matmul(dst, a[0], b[0], start=start, stop=False)
            pe.matmul(dst, a[1], b[0], start=False, stop=False)
            return pe.matmul(dst, a[0], b[1], start=False, stop=stop)

        def tok(h, l, kb, tb):
            return h[:, kb, tb * P:tb * P + P], l[:, kb, tb * P:tb * P + P]

        sets = (G, U, Y0, Y1), (T, X, S0, S1)
        tbanks = T, X, S1

        def score_banks(p, odd):
            return ((Y0, Y1), (T, X))[odd] if p == 0 else ((G, U), (Y0, Y1))[odd]

        block = ctx.enter_context(nc.Block())

        @block.sync
        def _(sp):
            for a in range(4):
                sp.dma_start(x[a % 2 * 64:a % 2 * 64 + 64, a // 2, :],
                             x_in[0].rearrange("(m a) d -> a m d", a=4)[a]).then_inc(x_in_done, 16)

            def load(t, item=0, src=None):
                if t >= RAW:
                    sp.wait_ge(lo_done, item * FFN_TILES + t - RAW + 1)
                if t == T_GROUP:
                    dst = raw[:, t % RAW].rearrange("p (b n) -> p b n", n=256)
                    src = a_w_group[0].rearrange("g (c p) n -> p (g c) n", p=P)
                else:
                    dst = raw[:, t % RAW].rearrange("p (k n) -> p k n", n=512)
                    src = (tile_source(t) if src is None else src).rearrange("(k p) n -> p k n", p=P)
                sp.dma_start(dst, src).then_inc(raw_full[t % RAW], 16)

            def load_rev(c):
                if c == 0:
                    sp.wait_ge(toep_out, 16)
                    sp.wait_ge(x_sum, 4)
                if c >= 2:
                    sp.wait_ge(bias_ready, 2 * (c - 1))
                for a in range(4):
                    src = bass.AP(toep_dram.tensor, 2 * c * 512 + a, [[4, 64], [512, 2], [1, S]])
                    sp.dma_start(biasrev[a % 2 * 64:a % 2 * 64 + 64, c % 2, a // 2], src).then_inc(rev_full[c % 2], 16)

            for t in range(T_MOE + CUT):
                load(t)
                for half in range(2):
                    t0 = T_ATT + half * HALF_TILES
                    for late in range(2):
                        if t == t0 + RAW + CUT + 6 * late:
                            load_rev(4 * half + 2 * late)
                            load_rev(4 * half + 2 * late + 1)

            def item_tiles(i, e, e_next=None):
                gu, dn = m_w_gate_up[0, bass.ds(e, 1)], m_w_down[0, bass.ds(e, 1)]
                gu, dn = gu.rearrange("o k n -> (o k) n"), dn.rearrange("o k n -> (o k) n")
                for t in range(CUT, FFN_TILES):
                    load(T_MOE + t, i, ffn_tile(gu, dn, t))
                if e_next is None:
                    return
                gu = m_w_gate_up[0, bass.ds(e_next, 1)].rearrange("o k n -> (o k) n")
                for t in range(CUT):
                    load(T_MOE + FFN_TILES + t, i, ffn_tile(gu, dn, t))

            with sp.Fori(0, E - 1) as i:
                item_tiles(i, i, i + 1)
            sp.wait_ge(ids_ready, 2)
            n_last = sp.value_load(ids[0:1, 0:1], min_val=E - 1, max_val=ITEMS - 1)
            with sp.Fori(E - 1, ITEMS - 1) as i:
                with sp.If(i < n_last):
                    e = sp.value_load(ids[0:1, bass.ds(i - (E - 2), 1)], min_val=0, max_val=E - 1)
                    e_next = sp.value_load(ids[0:1, bass.ds(i - (E - 3), 1)], min_val=0, max_val=E - 1)
                    item_tiles(i, e, e_next)
                with sp.Else():
                    sp.nop()
            item_tiles(n_last, sp.value_load(ids[0:1, bass.ds(n_last - (E - 2), 1)], min_val=0, max_val=E - 1))

            for a in range(4):
                if a % 2 == 0:
                    sp.wait_ge(out_ready[a // 2], 1)
                sp.dma_start(out[0].rearrange("(m a) d -> a m d", a=4)[a],
                             hn[a % 2 * 64:a % 2 * 64 + 64, a // 2, :]).then_inc(stored, 16)
            sp.wait_ge(stored, 64)

        @block.gpsimd
        def _(pool):
            pool.wait_ge(c_in[C_BAND], 16)
            pool.wait_ge(c_in[C_CLASS], 16)
            per_part = 2 * 2 * 2 * S
            for h in range(HEADS):
                c = h // 2
                if h % 2 == 0:
                    pool.wait_ge(rev_full[c % 2], 64 * (c // 2 + 1))
                if h >= 4:
                    pool.wait_ge(logit_done, h - 3)
                for qt in range(2):
                    base = ((c % 2 * 2 + qt) * 2 + h % 2) * S + S - 1
                    rev = lambda a0, na: bass.AP(biasrev[:].tensor, base - a0, [[per_part, P], [-1, na], [-4, 64]])
                    to = bias[:, h % 4, qt]
                    nc.gpsimd.tensor_tensor(to[:, 0:S].rearrange("p (a m) -> p a m", a=4), rev(0, 4),
                                            band[:, qt].rearrange("p (a m) -> p a m", a=4), ALU.add)
                    for g in range(2):
                        last = nc.gpsimd.tensor_tensor(
                            to[:, S + g * P:S + g * P + P].rearrange("p (a m) -> p a m", a=2), rev(2 * qt, 2),
                            classes[:, g].rearrange("p (a m) -> p a m", a=2), ALU.add)
                last.then_inc(bias_ready, 1)

            pool.wait_ge(x_sum, 8)
            pool.wait_ge(c_in[C_GAIN3], 16)
            for tb in range(NT):
                nc.gpsimd.tensor_tensor(hn[:, tb], x[:, tb], gain[:, 0], ALU.mult).then_inc(hn_done, 1)
            for t in (selT, yh, yl):
                last = nc.gpsimd.memset(t[:].bitcast(F32), 0.0)
            last.then_inc(y_lo, 1)

            pool.wait_ge(x_final, 1)
            pool.wait_ge(c_in[C_GAIN4], 16)
            nc.gpsimd.tensor_tensor(hn[:, 1], x[:, 1], gain[:, 1], ALU.mult).then_inc(hn_done, 1)

        @block.tensor
        def _(pe):
            def tile_ready(t, item=0):
                pe.wait_ge(lo_done, item * FFN_TILES + t + 1)

            def turn_x(n, kh):
                if n == 0:
                    pe.wait_ge(x_in_done, 64)
                else:
                    pe.wait_ge(x_sum, (2, 4, 8)[n - 1] - 1 + kh)
                for b, bank in ((0, G), (1, U)) if kh == 0 else ((2, T), (3, X)):
                    for kk in range(2):
                        for tb in range(NT):
                            mm = pe.transpose(bank[:, kk * S + tb * P:kk * S + tb * P + P],
                                              x[:, tb, (2 * b + kk) * P:(2 * b + kk + 1) * P], ident[:])
                    mm.then_inc(tx_psum, 1)

            def dense(t0, xh, xl, kbs, banks, after=(), amid=None):
                done = 0
                for n, ks in enumerate(kbs):
                    tile_ready(t0 + n)
                    for tb in range(NT):
                        if amid is not None and n == 0 and tb == 1:
                            amid()
                        for b, kb in enumerate(ks):
                            mm = mm3(pe, banks[tb][:], tok(xh, xl, kb, tb), wblk(t0 + n, b),
                                     start=done + b == 0, stop=n == len(kbs) - 1 and b == len(ks) - 1)
                    done += len(ks)
                    mm.then_inc(tile_used, 1)
                    if n < len(after):
                        after[n]()

            KH = [range(0, 4), range(4, 8)]

            pe.wait_ge(c_in[C_IDENT], 16)
            turn_x(0, 0)
            turn_x(0, 1)
            pe.wait_ge(tx_lo, 2)
            dense(T_IN, xTh, xTl, KH, (G, U), [lambda: pe.wait_ge(tx_lo, 4)])
            pe.wait_ge(c_in[C_BUCKET], 16)
            pe.wait_ge(c_in[C_RELB], 16)
            pe.matmul(S0[0:HEADS, :], relb[:], bucket[:], start=True, stop=True).then_inc(toep_psum, 1)
            dense(T_IN + 2, xTh, xTl, KH, (Y0, Y1))
            pe.wait_ge(u_act, 2)
            pe.wait_ge(u_dve, 2)
            pe.wait_ge(c_in[C_POOL], 16)
            pe.wait_ge(toep_sb, 1)
            for b, bank in enumerate((T, X, S0, S1)):
                for kk in range(2):
                    cb = 2 * b + kk
                    for tb in range(NT):
                        mm = pe.matmul(bank[:, kk * S:kk * S + S], u[:, tb, cb * P:cb * P + P],
                                       poolM[:, tb, cb // 2, :], start=tb == 0, stop=tb == NT - 1)
                mm.then_inc(mix_psum, 1)
            tile_ready(T_GROUP)
            for g, bank in enumerate((G, U, Y0, Y1)):
                pe.wait_ge(mix_lo, g + 1)
                for db in range(2):
                    for cb in range(2):
                        c = g * 512 + cb * S + db * P
                        w = whi[:, T_GROUP % CUT, c:c + P], wlo[:, T_GROUP % CUT, c:c + P]
                        r = mixTh[:, 2 * g + cb, :], mixTl[:, 2 * g + cb, :]
                        mm = mm3(pe, bank[:, db * S:db * S + S], w, r, start=cb == 0, stop=cb == 1)
                mm.then_inc(*((tile_used, 1) if g == 3 else (grp_psum, 1)))
            pe.wait_ge(grp_lo, 2)
            dense(T_OUT, yTh, yTl, KH, (T, X), [lambda: pe.wait_ge(grp_lo, 4)])
            dense(T_OUT + 2, yTh, yTl, KH, (Y0, Y1), [lambda: turn_x(1, 0)])

            pe.wait_ge(tx_lo, 6)

            def turn_hidden(j, width, src, ready):
                pe.wait_ge(h_ready, ready)
                for tb in range(width):
                    for c in range(4):
                        mm = pe.transpose((T, X)[tb][:, c * P:c * P + P], src(tb)[:, c * P:c * P + P], ident[:])
                    mm.then_inc(ht_psum, 1)

            for j in range(SLABS):
                t = T_FFN + 4 * j
                if j >= 1:
                    pe.wait_ge(silu_done, NT * j)
                if j == 0:
                    dense(t, xTh, xTl, KH, (G, S0), [lambda: pe.wait_ge(tx_lo, 8)], amid=lambda: turn_x(1, 1))
                else:
                    dense(t, xTh, xTl, KH, (G, S0))
                if j >= 1:
                    if j >= 2:
                        pe.wait_ge(ht_lo, NT * (j - 1))
                    turn_hidden(j - 1, NT, lambda tb: dh[:, tb], NT * j)
                dense(t + 2, xTh, xTl, KH, (U, S1))
            down = [range(4 * qn, 4 * qn + 4) for qn in range(DT)]
            acc = (Y0, Y1), (S0, S1)
            for n in range(2):
                for qn, ks in enumerate(down):
                    t = T_FFN + DOWN + DT * n + qn
                    if n == 0 and qn == 0:
                        pe.wait_ge(ht_lo, NT * (SLABS - 1))
                    if n == 0 and qn == 6:
                        pe.wait_ge(ht_lo, NT * SLABS)
                    tile_ready(t)
                    for tb in range(NT):
                        for b, kb in enumerate(ks):
                            mm = mm3(pe, acc[n][tb][:], (dTh[:, kb, tb], dTl[:, kb, tb]), wblk(t, b),
                                     start=kb == 0, stop=kb == KF - 1)
                    mm.then_inc(tile_used, 1)
                    if n == 0 and qn == 0:
                        turn_hidden(SLABS - 1, NT, lambda tb: dh[:, tb], NT * SLABS)
                    if n == 1 and qn == DT - 2:
                        turn_x(2, 0)

            pe.wait_ge(tx_lo, 10)

            def slab_read(n):
                if n % 3 == 2:
                    pe.wait_ge(pj_act, n // 3 + 1)
                else:
                    pe.wait_ge(pj_dve, n - n // 3 + 1)

            for half in range(2):
                t0 = T_ATT + half * HALF_TILES

                def scores(p):
                    pair = half * 4 + p
                    if p == 0:
                        slab_read(9 * half + 7)
                    else:
                        pe.wait_ge(logit_done, 2 * pair)
                    if p == 1:
                        slab_read(9 * half + 8)
                    for qt in range(2):
                        for g in range(3):
                            cols = slice(0, S) if g == 0 else slice(qt * P, qt * P + P)
                            to = slice(0, S) if g == 0 else slice(S + (g - 1) * P, S + g * P)
                            for odd in range(2):
                                r = odd * HD
                                mm = pe.matmul(score_banks(p, odd)[qt][:, to], q[r:r + HD, g, p, qt * P:qt * P + P],
                                               k[r:r + HD, g, p, cols], start=True, stop=True)
                    mm.then_inc(qk_done, 1)

                def project(n, tb, blocks):
                    tile_ready(t0 + 18 + n)
                    for b in blocks:
                        mm = mm3(pe, ((G, U), (Y0, Y1))[n][tb][:], tok(oTh, oTl, b, tb), wblk(t0 + 18 + n, b),
                                 start=b == 0, stop=b == 3)
                    return mm

                for s in range(9):
                    n = half * 9 + s
                    banks = sets[s % 2]
                    if s >= 2:
                        slab_read(n - 2)
                    if n == 1:
                        pe.wait_ge(rcols_done, 1)
                    if half == 1 and s == 0:
                        pe.wait_ge(x_sum, 5)
                    if s % 3 == 2:
                        dense(t0 + 2 * s, xTh, xTl, KH, banks, [lambda: scores(0)] if s == 8 else ())
                        continue
                    for kh in range(2):
                        tile_ready(t0 + 2 * s + kh)
                        for cb in range(4):
                            if n == 0 and kh == 0 and cb == 2:
                                turn_x(2, 1)
                            if half == 1 and s == 0 and kh == 0 and cb == 2:
                                pe.wait_ge(x_sum, 6)
                            if n == 0 and kh == 1 and cb == 2:
                                pe.wait_ge(rdiag_done, 1)
                                for tb in range(NT):
                                    mm = pe.matmul(S1[:, tb * P:tb * P + P], tri[:, 1], rdiag[:, tb], start=True, stop=True)
                                mm.then_inc(rcols_psum, 1)
                            for b in range(4):
                                kb = 4 * kh + b
                                h_, l_ = wblk(t0 + 2 * s + kh, b)
                                mm = mm3(pe, banks[cb][:, 0:S], (h_[:, cb * P:cb * P + P], l_[:, cb * P:cb * P + P]),
                                         (xTh[:, kb], xTl[:, kb]), start=kb == 0, stop=kb == KD - 1)
                        mm.then_inc(tile_used, 1)
                        if n == 0 and kh == 0:
                            pe.wait_ge(tx_lo, 12)
                for p in range(HH // 2):
                    pair = half * 4 + p
                    for unit in range(4):
                        odd, qt = divmod(unit, 2)
                        n = 4 * pair + unit
                        if qt == 0:
                            pe.wait_ge(prob_done, 2 * pair + odd + 1)
                        if n >= 3:
                            pe.wait_ge(pT_sb, n - 2)
                        for c in range(4):
                            mm = pe.transpose(tbanks[n % 3][:, c * P:c * P + P], logit[:, odd, qt, c * P:c * P + P], ident[:])
                        mm.then_inc(pT_psum, 1)
                        if p == HH // 2 - 1 and qt == 1:
                            if odd == 0:
                                pe.wait_ge(o_lo, pair)
                            project(0, odd, range(3))
                    if p == 0:
                        scores(1)
                    pe.wait_ge(pT_sb, 4 * pair + 4)
                    if pair >= 1:
                        pe.wait_ge(o_lo, pair)
                    for kt in range(NT):
                        for odd in range(2):
                            h, r = 2 * p + odd, odd * HD
                            pe.matmul(S0[r:r + HD, 0:S].rearrange("p (a b) -> p a b", a=2), v[:, kt, 0, h * HD:h * HD + HD],
                                      probsT[:, odd, :, kt * P:kt * P + P], start=kt == 0, stop=False, skip_group_check=True)
                    for qt in range(2):
                        for g in (1, 2):
                            for odd in range(2):
                                h, r = 2 * p + odd, odd * HD
                                mm = pe.matmul(S0[r:r + HD, qt * P:qt * P + P], v[:, qt, g, h * HD:h * HD + HD],
                                               probsT[:, odd, qt, S + (g - 1) * P:S + g * P], start=False,
                                               stop=g == 2, skip_group_check=True)
                    mm.then_inc(pv_done, 1)
                    if p + 2 < HH // 2:
                        scores(p + 2)
                project(1, 0, range(3))
                pe.wait_ge(o_lo, 4 * half + 4)
                project(0, 0, [3])
                project(0, 1, [3]).then_inc(tile_used, 1)
                project(1, 1, range(4))
                if half == 1:
                    turn_x(3, 0)
                project(1, 0, [3]).then_inc(tile_used, 1)

            turn_x(3, 1)
            pe.wait_ge(rt_lo, 1)
            pe.wait_ge(tx_lo, 14)
            for kb in range(KD):
                if kb == KD // 2:
                    pe.wait_ge(tx_lo, 16)
                mm = mm3(pe, Y0[0:E, 0:S], (routh[:, kb], routl[:, kb]), (xTh[:, kb], xTl[:, kb]),
                         start=kb == 0, stop=kb == KD - 1)
            mm.then_inc(lt_psum, 1)
            pe.wait_ge(lt_sb, 1)
            for tb in range(NT):
                mm = pe.transpose(Y0[:, tb * E:tb * E + E], logitsT[:, tb * P:tb * P + P], ident[0:E, 0:E])
            mm.then_inc(logits_psum, 1)
            pe.wait_ge(c_in[C_TRI], 16)
            pe.wait_ge(sel_ready, 1)
            chosen = tiny[:, 4, :]
            pe.matmul(Y1[:, 0:2 * E], tri[:, 0], chosen, start=True, stop=True)
            pe.matmul(Y1[:, 2 * E:4 * E], tri[:, 1], chosen, start=True, stop=True).then_inc(rank_psum, 1)

            def gather(n, rounds):
                for r in rounds:
                    bank, src = (G, U, T, X)[r], (hnh, hnl)[r // 2]
                    for kk in range(4):
                        kb = r % 2 * 4 + kk
                        for tb in range(NT):
                            mm = pe.matmul(bank[:, kk * P:kk * P + P], src[:, tb, kb * P:kb * P + P], sel[:, tb, :],
                                           start=tb == 0, stop=tb == NT - 1)
                    mm.then_inc(ga_psum, 1)

            pe.wait_ge(hnh_done, 2)
            pe.wait_ge(pick_ready, 1)
            gather(0, (0, 1))
            pe.wait_ge(hnl_done, 2)
            gather(0, (2, 3))
            pe.wait_ge(ids_ready, 1)
            n_last = pe.value_load(ids[0:1, 0:1], min_val=E - 1, max_val=ITEMS - 1)

            def spread(n, count):
                pe.wait_ge(y_lo, count + 1)
                pe.wait_ge(x_added, count + 1)
                for tb in range(NT):
                    bank = (S0, S1)[tb]
                    pe.matmul(bank[:], selT[:, tb], yh[:, n * 512:n * 512 + 512], start=True, stop=False)
                    mm = pe.matmul(bank[:], selT[:, tb], yl[:, n * 512:n * 512 + 512], start=False, stop=True)
                mm.then_inc(sc_psum, 1)

            def item_body(i, last=False):
                pe.wait_ge(ga_sb, i * 4 + 3)

                def product(t, xh, xl, ks, bank, stop):
                    tile_ready(T_MOE + t, i)
                    for b, kb in enumerate(ks):
                        mm = mm3(pe, bank[:], (xh[:, kb], xl[:, kb]), wblk(T_MOE + t, b), start=kb == 0,
                                 stop=stop and b == len(ks) - 1)
                    mm.then_inc(tile_used, 1)

                for j in range(SLABS):
                    if j >= 1:
                        pe.wait_ge(silu_done, i * SLABS + PAIRS0 + j)
                    product(4 * j, eTh, eTl, KH[0], G, False)
                    if j == 0:
                        pe.wait_ge(ga_sb, i * 4 + 4)
                    product(4 * j + 1, eTh, eTl, KH[1], G, True)
                    if j == 0:
                        spread(1, i * 2)
                    if j >= 1:
                        pe.wait_ge(ht_lo, i * SLABS + PAIRS0 + j - 1)
                        turn_hidden(j - 1, 1, lambda tb: mh, i * SLABS + PAIRS0 + j)
                    if j == 1:
                        for tb in range(NT):
                            mm = pe.transpose(X[:, tb * P:tb * P + P], sel[:, tb, :].bitcast(F32), ident[:])
                        mm.then_inc(selT_psum, 1)
                    product(4 * j + 2, eTh, eTl, KH[0], U, False)
                    product(4 * j + 3, eTh, eTl, KH[1], U, True)
                for n in range(2):
                    for qn, ks in enumerate(down):
                        if n == 0 and qn == 0:
                            pe.wait_ge(ht_lo, i * SLABS + PAIRS0 + SLABS - 1)
                        if n == 0 and qn == DT - 1:
                            pe.wait_ge(ht_lo, i * SLABS + PAIRS0 + SLABS)
                        product(DOWN + DT * n + qn, hTh, hTl, ks, (Y0, Y1)[n], qn == DT - 1)
                        if n == 0 and qn == 0:
                            turn_hidden(SLABS - 1, 1, lambda tb: mh, i * SLABS + PAIRS0 + SLABS)
                        if n == 1 and qn == 1:
                            pe.wait_ge(selT_ready, i + 1)
                            spread(0, i * 2 + 1)
                        if n == 1 and qn == 2 and not last:
                            pe.wait_ge(pick_ready, i + 2)
                            gather(i + 1, (0, 1))
                        if n == 1 and qn == 3 and not last:
                            gather(i + 1, (2, 3))

            with pe.Fori(0, ITEMS - 1) as i:
                with pe.If(i < n_last):
                    item_body(i)
                with pe.Else():
                    pe.nop()
            item_body(n_last, last=True)
            pe.wait_ge(y_hi, n_last * 2 + 2)
            pe.wait_ge(x_added, n_last * 2 + 3)
            for part, y in enumerate((yh, yl)):
                if part == 1:
                    pe.wait_ge(y_lo, n_last * 2 + 3)
                for tb in (1, 0):
                    mm = pe.matmul((S0, S1)[tb][:], selT[:, tb], y[:, 512:D], start=part == 0, stop=part == 1)
            mm.then_inc(sc_psum, 1)

        @block.scalar
        def _(act):
            def load_const(ns):
                for n in ns:
                    act.dma_start(*CONST[n]).then_inc(c_in[n], 16)

            def copy(dst, src, s, scale=1.0):
                return nc.scalar.activation(dst, src, ACT.Copy, scale=scale).then_inc(s, 1)

            def root(n):
                nc.scalar.activation(small[:, 9:10], ident[:, 0:1], ACT.Sqrt)
                act.wait_ge(*((x_in_done, 64) if n == 0 else (x_final, 1) if n == 4 else (x_sum, (2, 4, 8)[n - 1])))
                nc.scalar.activation((hn, squares)[n >= 3][:, 1], x[:, 1], ACT.Square, accum_out=ss[:, 1:2]).then_inc(sq_done, 1)
                act.wait_ge(ms_done, n + 1)
                nc.scalar.activation(std, ms, ACT.Sqrt).then_inc(std_done, 1)

            def cut_x(n, kh):
                for b, bank in ((0, G), (1, U)) if kh == 0 else ((2, T), (3, X)):
                    act.wait_ge(tx_psum, 4 * n + b + 1)
                    for kk in range(2):
                        kb = 2 * b + kk
                        last = nc.scalar.activation(xTh[:, kb], bank[:, kk * S:kk * S + S], ACT.Copy,
                                                    scale=gainT[:, n, kb:kb + 1])
                    last.then_inc(tx_hi, 1)

            def ahead(t):
                make_hi(act, t + CUT)

            load_const((C_IDENT, C_GAINT))
            act.wait_ge(c_in[C_IDENT], 16)
            act.wait_ge(c_in[C_GAINT], 16)
            nc.scalar.activation(small[:, 8:9], gainT[:, 0, 0:1], ACT.Copy)
            cut_x(0, 0)
            load_const((C_BUCKET, C_RELB, C_SCALE))
            make_hi(act, 0)
            cut_x(0, 1)
            for t in range(1, CUT):
                make_hi(act, t)
            load_const((C_POOL,))
            root(0)
            act.wait_ge(rstd_done, 1)
            for n in range(2):
                ahead(2 * n)
                act.wait_ge(tile_used, 2 * n + 2)
                copy(u[:, 0, n * 512:n * 512 + 512], ((G, Y0)[n])[:], u_act, scale=rstd[:, 0:1])
                ahead(2 * n + 1)
                if n == 0:
                    act.wait_ge(toep_psum, 1)
                    copy(toep[:], S0[0:HEADS, :], toep_sb, scale=-1.0)
            for b, bank in enumerate((T, X, S0, S1)):
                act.wait_ge(mix_psum, b + 1)
                copy(mixTh[:, 2 * b:2 * b + 2, :].rearrange("p k s -> p (k s)"), bank[:], mix_hi)
            act.wait_ge(toep_sb, 1)
            act.dma_start(toep_dram, toep[:]).then_inc(toep_out, 16)
            act.wait_ge(c_in[C_SCALE], 16)
            for g, bank in enumerate((G, U, Y0, Y1)):
                if g < 3:
                    act.wait_ge(grp_psum, g + 1)
                else:
                    act.wait_ge(tile_used, T_GROUP + 1)
                for db in range(2):
                    last = nc.scalar.activation(yTh[:, 2 * g + db, :], bank[:, db * S:db * S + S], ACT.Copy,
                                                scale=scaleT[:, 2 * g + db:2 * g + db + 1])
                last.then_inc(grp_hi, 1)
            load_const((C_BAND, C_CLASS, C_TRI, C_IOTA, C_ROUTER))
            for t in range(T_GROUP, T_OUT + 3):
                ahead(t)
            cut_x(1, 0)
            ahead(T_OUT + 3)

            cut_x(1, 1)
            root(1)
            act.wait_ge(toep_out, 16)
            act.wait_ge(rstd_done, 2)
            for j in range(SLABS):
                t = T_FFN + 4 * j
                ahead(t)
                for tb in range(NT):
                    act.wait_ge(tile_used, t + 2)
                    if j >= 1:
                        act.wait_ge(h_ready, NT * j)
                    nc.scalar.activation(dsilu[:, tb], (G, S0)[tb][:], ACT.Silu, scale=rstd[:, tb:tb + 1]
                                         ).then_inc(silu_done, 1)
                ahead(t + 1)
                if j >= 1:
                    for tb in range(NT):
                        act.wait_ge(ht_psum, NT * (j - 1) + tb + 1)
                        copy(dTh[:, 4 * j - 4:4 * j, tb], (T, X)[tb][:].rearrange("p (c t) -> p c t", c=4), ht_hi)
                ahead(t + 2)
                ahead(t + 3)
            for t in range(DOWN, FFN_TILES):
                ahead(T_FFN + t)
                if t == DOWN:
                    for tb in range(NT):
                        act.wait_ge(ht_psum, NT * (SLABS - 1) + tb + 1)
                        copy(dTh[:, KF - 4:KF, tb], (T, X)[tb][:].rearrange("p (c t) -> p c t", c=4), ht_hi)
                if t == FFN_TILES - 2:
                    cut_x(2, 0)

            cut_x(2, 1)
            act.wait_ge(c_in[C_ROUTER], 16)
            copy(routh[:], router[:], rt_hi)
            root(2)
            act.wait_ge(rstd_done, 3)
            for half in range(2):
                t0 = T_ATT + half * HALF_TILES

                def exps(h):
                    act.wait_ge(logit_done, half * HH + h + 1)
                    for qt in range(2):
                        last = nc.scalar.activation(logit[:, h % 2, qt], logit[:, h % 2, qt], ACT.Exp, scale=-1.0,
                                                    bias=nmin[:, h % 2, qt:qt + 1], accum_out=rsum[:, h % 2, qt:qt + 1])
                    last.then_inc(exp_done, 1)

                for s in range(9):
                    ahead(t0 + 2 * s)
                    if s == 8:
                        exps(0)
                        exps(1)
                    if s % 3 == 2:
                        act.wait_ge(tile_used, t0 + 2 * s + 2)
                        for tb in range(NT):
                            last = nc.scalar.activation(v[:, tb, s // 3], sets[s % 2][tb][:], ACT.Copy,
                                                        scale=rstd[:, tb:tb + 1])
                        last.then_inc(pj_act, 1)
                    if s < 8:
                        ahead(t0 + 2 * s + 1)

                for p in range(HH // 2):
                    pair = half * 4 + p
                    for unit in range(4):
                        n = 4 * pair + unit
                        act.wait_ge(pT_psum, n + 1)
                        if unit == 0 and pair >= 1:
                            act.wait_ge(pv_done, pair)
                        copy(probsT[:, unit // 2, unit % 2], tbanks[n % 3][:], pT_sb)
                    if p + 1 < HH // 2:
                        exps(2 * p + 2)
                        exps(2 * p + 3)
                    if p == HH // 2 - 1:
                        ahead(t0 + 17)
                    act.wait_ge(pv_done, pair + 1)
                    copy(oTh[:, p], S0[:, 0:S], o_hi)
                if half == 1:
                    act.wait_ge(bias_ready, HEADS)
                    load_const((C_GAIN3, C_GAIN4))
                ahead(t0 + 18)
                if half == 0:
                    ahead(t0 + 19)

            cut_x(3, 0)
            cut_x(3, 1)
            root(3)
            act.wait_ge(rstd_done, 4)
            for tb in range(NT):
                act.wait_ge(hn_done, tb + 1)
                copy(hnh[:, tb], hn[:, tb], hnh_done, scale=rstd[:, tb:tb + 1])
            act.wait_ge(gap_done, 1)
            for tb in range(NT):
                last = nc.scalar.activation(tiny[:, 1, tb:tb + 1], tiny[:, 0, tb:tb + 1], ACT.Exp, scale=rstd[:, tb:tb + 1])
            last.then_inc(e_done, 1)
            ahead(T_MOE - 1)

            def cut_tokens(n):
                for r, bank in enumerate((G, U, T, X)):
                    act.wait_ge(ga_psum, 4 * n + r + 1)
                    copy((eTh, eTl)[r // 2][:, r % 2 * 4:r % 2 * 4 + 4].rearrange("p k t -> p (k t)"), bank[:], ga_sb)

            cut_tokens(0)
            act.wait_ge(ids_ready, 1)
            n_last = act.value_load(ids[0:1, 0:1], min_val=E - 1, max_val=ITEMS - 1)

            def item_body(i, last=False):
                nc.scalar.activation(small[:, 10:11], ident[:, 0:1], ACT.Silu)
                def ahead(t):
                    if not last or t + CUT < FFN_TILES:
                        make_hi(act, T_MOE + t + CUT, i)

                def hidden_hi(j):
                    act.wait_ge(ht_psum, i * SLABS + PAIRS0 + j + 1)
                    copy(hTh[:, 4 * j:4 * j + 4].rearrange("p c t -> p (c t)"), T[:], ht_hi)

                def y_cut(n):
                    act.wait_ge(tile_used, i * FFN_TILES + T_MOE + DOWN + DT * n + DT)
                    copy(yh[:, n * 512:n * 512 + 512], (Y0, Y1)[n][:], y_hi)

                for j in range(SLABS):
                    ahead(4 * j)
                    act.wait_ge(tile_used, i * FFN_TILES + T_MOE + 4 * j + 2)
                    act.wait_ge(h_ready, i * SLABS + PAIRS0 + j)
                    nc.scalar.activation(msilu, G[:], ACT.Silu).then_inc(silu_done, 1)
                    ahead(4 * j + 1)
                    if j >= 1:
                        hidden_hi(j - 1)
                    ahead(4 * j + 2)
                    if j == 1:
                        act.wait_ge(selT_psum, i + 1)
                        copy(selT[:].rearrange("p t s -> p (t s)"), X[:, 0:S], selT_ready)
                    ahead(4 * j + 3)
                for t in range(DOWN, FFN_TILES):
                    if t == FFN_TILES - 1:
                        y_cut(1)
                    ahead(t)
                    if t == DOWN:
                        hidden_hi(SLABS - 1)
                    if t == DOWN + DT - 1:
                        y_cut(0)
                    if t == DOWN + DT + 3 and not last:
                        cut_tokens(i + 1)

            with act.Fori(0, ITEMS - 1) as i:
                with act.If(i < n_last):
                    item_body(i)
                with act.Else():
                    act.nop()
            item_body(n_last, last=True)
            root(4)
            act.wait_ge(rstd_done, 5)
            act.wait_ge(hn_done, 3)
            copy(hn[:, 1], hn[:, 1], out_ready[1], scale=rstd[:, 1:2])

        @block.vector
        def _(dve):
            links, sums = [0], [0]

            def link(ins):
                links[0] += 1
                ins.then_inc(chain, 1)
                dve.wait_ge(chain, links[0])

            def stats(n, between=lambda: None):
                link(nc.vector.tensor_tensor_reduce((hn, squares)[n >= 3][:, 0], x[:, 0], x[:, 0], 1.0, 0.0, ALU.mult, ALU.add,
                                                    accum_out=ss[:, 0:1]))
                dve.wait_ge(sq_done, n + 1)
                nc.vector.tensor_scalar(ms, ss, 1.0 / D, EPS, ALU.mult, ALU.add).then_inc(ms_done, 1)
                between()
                dve.wait_ge(std_done, n + 1)
                nc.vector.reciprocal(rstd, std).then_inc(rstd_done, 1)
                dve.wait_ge(rstd_done, n + 1)

            def lo(dst, src, hi, s):
                return nc.vector.tensor_tensor(dst, src, hi.bitcast(F32), ALU.subtract).then_inc(s, 1)

            def cut_x(n, kh):
                for b, bank in ((0, G), (1, U)) if kh == 0 else ((2, T), (3, X)):
                    dve.wait_ge(tx_hi, 4 * n + b + 1)
                    for kk in range(2):
                        kb = 2 * b + kk
                        last = nc.vector.scalar_tensor_tensor(xTl[:, kb], bank[:, kk * S:kk * S + S], gainT[:, n, kb:kb + 1],
                                                              xTh[:, kb].bitcast(F32), ALU.mult, ALU.subtract)
                    last.then_inc(tx_lo, 1)

            def ahead(t):
                make_lo(dve, t + CUT)

            def add_x(n, banks):
                for tb in range(NT):
                    sl = x[:, tb, n * 512:n * 512 + 512]
                    last = nc.vector.tensor_tensor(sl, banks[tb][:], sl, ALU.add)
                last.then_inc(x_sum, 1)
                sums[0] += 1
                dve.wait_ge(x_sum, sums[0])

            cut_x(0, 0)
            make_lo(dve, 0)
            cut_x(0, 1)
            for t in range(1, CUT):
                make_lo(dve, t)
            dve.wait_ge(x_in_done, 64)
            stats(0)
            for n in range(2):
                ahead(2 * n)
                dve.wait_ge(tile_used, 2 * n + 2)
                nc.vector.tensor_scalar(u[:, 1, n * 512:n * 512 + 512], ((U, Y1)[n])[:], rstd[:, 1:2], None,
                                        ALU.mult).then_inc(u_dve, 1)
                ahead(2 * n + 1)
            for b, bank in enumerate((T, X, S0, S1)):
                dve.wait_ge(mix_hi, b + 1)
                f = lambda t: t[:, 2 * b:2 * b + 2, :].rearrange("p k s -> p (k s)")
                lo(f(mixTl), bank[:], f(mixTh), mix_lo)
            for g, bank in enumerate((G, U, Y0, Y1)):
                dve.wait_ge(grp_hi, g + 1)
                for db in range(2):
                    last = nc.vector.scalar_tensor_tensor(
                        yTl[:, 2 * g + db], bank[:, db * S:db * S + S], scaleT[:, 2 * g + db:2 * g + db + 1],
                        yTh[:, 2 * g + db].bitcast(F32), ALU.mult, ALU.subtract)
                last.then_inc(grp_lo, 1)
            for t in range(T_GROUP, T_OUT + 2):
                ahead(t)
            add_x(0, (T, X))
            ahead(T_OUT + 2)
            cut_x(1, 0)
            dve.wait_ge(tile_used, T_FFN)
            add_x(1, (Y0, Y1))

            cut_x(1, 1)
            ahead(T_OUT + 3)
            stats(1)
            for j in range(SLABS):
                t = T_FFN + 4 * j
                ahead(t)
                ahead(t + 1)
                if j >= 1:
                    for tb in range(NT):
                        dve.wait_ge(ht_hi, NT * (j - 1) + tb + 1)
                        lo(dTl[:, 4 * j - 4:4 * j, tb], (T, X)[tb][:].rearrange("p (c t) -> p c t", c=4),
                           dTh[:, 4 * j - 4:4 * j, tb], ht_lo)
                ahead(t + 2)
                dve.wait_ge(tile_used, t + 4)
                for tb in range(NT):
                    dve.wait_ge(silu_done, NT * j + tb + 1)
                    if j >= 1:
                        dve.wait_ge(ht_psum, NT * j)
                    nc.vector.scalar_tensor_tensor(dh[:, tb], (U, S1)[tb][:], rstd[:, tb:tb + 1], dsilu[:, tb],
                                                   ALU.mult, ALU.mult).then_inc(h_ready, 1)
                ahead(t + 3)
            for t in range(DOWN, FFN_TILES):
                if t < FFN_TILES - 1:
                    ahead(T_FFN + t)
                if t == DOWN:
                    for tb in range(NT):
                        dve.wait_ge(ht_hi, NT * (SLABS - 1) + tb + 1)
                        lo(dTl[:, KF - 4:KF, tb], (T, X)[tb][:].rearrange("p (c t) -> p c t", c=4),
                           dTh[:, KF - 4:KF, tb], ht_lo)
                if t == DOWN + DT - 1:
                    add_x(0, (Y0, Y1))
                if t == FFN_TILES - 2:
                    cut_x(2, 0)
            dve.wait_ge(tile_used, T_ATT)
            add_x(1, (S0, S1))

            cut_x(2, 1)
            stats(2)
            for tb in range(NT):
                last = nc.vector.tensor_scalar(rdiag[:, tb], ident[:], rstd[:, tb:tb + 1], None, ALU.mult)
            last.then_inc(rdiag_done, 1)
            ahead(T_ATT - 1)
            dve.wait_ge(rt_hi, 1)
            lo(routl[:], router[:], routh[:], rt_lo)
            for half in range(2):
                t0 = T_ATT + half * HALF_TILES
                for s in range(9):
                    g, kind = divmod(s, 3)
                    if half == 0 and s == 0:
                        dve.wait_ge(rcols_psum, 1)
                        nc.vector.tensor_copy(rcols[:], S1[:, 0:S]).then_inc(rcols_done, 1)
                        dve.wait_ge(rcols_done, 1)
                    ahead(t0 + 2 * s)
                    if kind < 2:
                        dve.wait_ge(tile_used, t0 + 2 * s + 2)
                        for cb in range(4):
                            last = nc.vector.scalar_tensor_tensor((q, k)[kind][:, g, cb], sets[s % 2][cb][:, 0:S],
                                                                  (-0.125, 1.0)[kind], rcols[:], ALU.mult, ALU.mult)
                        last.then_inc(pj_dve, 1)
                    if s < 8:
                        ahead(t0 + 2 * s + 1)

                def logits(h):
                    head = half * HH + h
                    dve.wait_ge(qk_done, head // 2 + 1)
                    dve.wait_ge(bias_ready, head + 1)
                    if h >= 2:
                        dve.wait_ge(pT_psum, 2 * head - 2)
                    for qt in range(2):
                        last = nc.vector.tensor_tensor_reduce(
                            logit[:, h % 2, qt], score_banks(h // 2, h % 2)[qt][:], bias[:, h % 4, qt], 1.0, 3.0e38,
                            ALU.add, ALU.min, accum_out=nmin[:, h % 2, qt:qt + 1])
                    last.then_inc(logit_done, 1)

                def norm_probs(h):
                    dve.wait_ge(exp_done, half * HH + h + 1)
                    link(nc.vector.reciprocal(rinv[:, h % 2], rsum[:, h % 2]))
                    for qt in range(2):
                        last = nc.vector.tensor_scalar(logit[:, h % 2, qt], logit[:, h % 2, qt],
                                                       rinv[:, h % 2, qt:qt + 1], None, ALU.mult)
                    last.then_inc(prob_done, 1)

                def cut_o(p):
                    dve.wait_ge(o_hi, half * 4 + p + 1)
                    lo(oTl[:, p], S0[:, 0:S], oTh[:, p], o_lo)

                logits(0)
                logits(1)
                for p in range(HH // 2):
                    norm_probs(2 * p)
                    if p >= 1:
                        cut_o(p - 1)
                    norm_probs(2 * p + 1)
                    if p + 1 < HH // 2:
                        logits(2 * p + 2)
                        logits(2 * p + 3)
                ahead(t0 + 17)
                cut_o(HH // 2 - 1)
                dve.wait_ge(tile_used, t0 + 19)
                add_x(0, (G, U))
                if half == 0:
                    ahead(t0 + 18)
                dve.wait_ge(tile_used, t0 + 20)
                add_x(1, (Y0, Y1))
                if half == 0:
                    ahead(t0 + 19)

            cut_x(3, 0)
            cut_x(3, 1)

            def logits_to_sbuf():
                dve.wait_ge(lt_psum, 1)
                nc.vector.tensor_copy(logitsT, Y0[0:E, 0:S]).then_inc(lt_sb, 1)

            stats(3, logits_to_sbuf)
            gap, ex, gates, chosen, picked, gatev = (tiny[:, i, :] for i in (0, 1, 2, 4, 5, 6))
            logs, best, idxf = tiny[:, 7, :], tiny[:, 8, :], tiny[:, 9, 0:4]
            places, over_place, full, kth, mask = (tiny[:, i, :] for i in (10, 11, 12, 13, 14))
            eid, totals = tiny[:, 3, :], tiny[:, 15, :]
            two = lambda t: t.rearrange("p (t e) -> p t e", e=E)
            dve.wait_ge(logits_psum, 1)
            link(nc.vector.tensor_copy(logs, Y0[:, 0:2 * E]))
            for tb in range(NT):
                last = nc.vector.max(best[:, tb * 8:tb * 8 + 8], logs[:, tb * 8:tb * 8 + 8])
            link(last)
            nc.vector.tensor_tensor(gap[:, 0:2], two(best)[:, :, 1], two(best)[:, :, 0], ALU.subtract).then_inc(gap_done, 1)
            for tb in range(NT):
                last = nc.vector.max_index(idx[:, tb], best[:, tb * 8:tb * 8 + 8], logs[:, tb * 8:tb * 8 + 8])
            link(last)
            link(nc.vector.tensor_copy(idxf.rearrange("p (t c) -> p t c", c=2), idx[:, :, 0:2]))
            dve.wait_ge(c_in[C_IOTA], 16)
            first, second = picked, gatev
            for tb in range(NT):
                sl = slice(tb * 8, tb * 8 + 8)
                nc.vector.tensor_scalar(first[:, sl], iota[:, P:P + 8], idxf[:, 2 * tb:2 * tb + 1], None, ALU.is_equal)
                last = nc.vector.tensor_scalar(second[:, sl], iota[:, P:P + 8], idxf[:, 2 * tb + 1:2 * tb + 2], None, ALU.is_equal)
            link(last)
            nc.vector.tensor_tensor(chosen, first, second, ALU.add).then_inc(sel_ready, 1)

            def tokens_cut(tb):
                dve.wait_ge(hnh_done, tb + 1)
                nc.vector.scalar_tensor_tensor(hnl[:, tb], hn[:, tb], rstd[:, tb:tb + 1], hnh[:, tb].bitcast(F32),
                                               ALU.mult, ALU.subtract).then_inc(hnl_done, 1)

            dve.wait_ge(rank_psum, 1)
            nc.vector.tensor_copy(places[:, 0:E], Y1[:, 0:E])
            link(nc.vector.tensor_copy(totals, Y1[:, 2 * E:4 * E]))
            link(nc.vector.tensor_tensor(places[:, E:2 * E], Y1[:, E:2 * E], totals[:, 0:E], ALU.add))
            for tb in range(NT):
                sl = slice(tb * 8, tb * 8 + 8)
                last = nc.vector.scalar_tensor_tensor(rank_item[:, tb, 0:E], places[:, sl], SHIFT, chosen[:, sl],
                                                      ALU.add, ALU.mult)
            link(last)

            def pick(n):
                for tb in range(NT):
                    last = nc.vector.tensor_scalar(sel[:, tb], iota[:, 0:P], rank_item[:, tb, bass.ds(n, 1)], None, ALU.is_equal)
                last.then_inc(pick_ready, 1)

            pick(0)
            tokens_cut(0)
            tokens_cut(1)
            nc.vector.memset(kth, 0.0)
            nc.vector.memset(full, 0.0)
            link(nc.vector.memset(mask, 0.0))
            link(nc.vector.tensor_tensor(mask[:, 8:16], totals[:, 0:E], totals[:, E:2 * E], ALU.add))
            link(nc.vector.tensor_scalar(full[:, 8:16], mask[:, 8:16], float(CAP), None, ALU.is_gt))
            link(nc.vector.tensor_tensor(kth[:, 8:16], full[:, 8:16], full[:, 7:15], ALU.add))
            link(nc.vector.tensor_tensor(mask[:, 8:16], kth[:, 8:16], kth[:, 6:14], ALU.add))
            link(nc.vector.tensor_tensor(kth[:, 8:16], mask[:, 8:16], mask[:, 4:12], ALU.add))
            link(nc.vector.tensor_scalar(eid[:, 0:1], kth[:, 15:16], float(E - 1), None, ALU.add))
            link(nc.vector.tensor_copy(ids[:, 0:1], eid[:, 0:1]))
            nc.vector.tensor_tensor(kth[:, 0:8], kth[:, 8:16], full[:, 8:16], ALU.mult).then_inc(ids_ready, 1)
            ahead(T_MOE - 2)
            ahead(T_MOE - 1)
            for tb in range(NT):
                sl = slice(tb * 8, tb * 8 + 8)
                nc.vector.scalar_tensor_tensor(over_place[:, sl], places[:, sl], SHIFT - CAP, chosen[:, sl], ALU.add, ALU.mult)
            nc.vector.memset(eid[:, 2 + OVER:3 + OVER], 0.0)
            nc.vector.memset(eid[:, 1:2], float(E - 1))
            nc.vector.memset(gate_item[:, :, 0:1], 0.0)
            dve.wait_ge(e_done, 1)
            link(nc.vector.tensor_scalar(gates[:, 0:2], ex[:, 0:2], 1.0, None, ALU.add))
            link(nc.vector.reciprocal(gates[:, 2:4], gates[:, 0:2]))
            link(nc.vector.tensor_tensor(gates[:, 4:6], ex[:, 0:2], gates[:, 2:4], ALU.mult))
            for tb in range(NT):
                sl = slice(tb * 8, tb * 8 + 8)
                last = nc.vector.tensor_scalar(scrap[:, tb], first[:, sl], gates[:, 2 + tb:3 + tb], None, ALU.mult)
            link(last)
            for tb in range(NT):
                sl = slice(tb * 8, tb * 8 + 8)
                last = nc.vector.scalar_tensor_tensor(gate_item[:, tb, 1:E + 1], second[:, sl], gates[:, 4 + tb:5 + tb],
                                                      scrap[:, tb], ALU.mult, ALU.add)
            link(last)

            for n in range(OVER):
                link(nc.vector.tensor_scalar(mask[:, 0:8], kth[:, 0:8], float(n + 1), None, ALU.is_equal))
                picks = [(iota[:, P:P + 8], eid[:, 2 + n:3 + n])]
                for tb in range(NT):
                    sl = slice(tb * 8, tb * 8 + 8)
                    picks += [(over_place[:, sl], rank_item[:, tb, E + n:E + n + 1]),
                              (gate_item[:, tb, 1:E + 1], gate_item[:, tb, E + n + 1:E + n + 2])]
                for i, (src, dst) in enumerate(picks):
                    last = nc.vector.tensor_tensor_reduce(scrap[:, 2 + 5 * n + i], mask[:, 0:8], src, 1.0, 0.0, ALU.mult,
                                                          ALU.add, accum_out=dst)
                link(last)
            nc.vector.tensor_copy(ids[:, 1:3 + OVER], eid[:, 1:3 + OVER]).then_inc(ids_ready, 1)
            dve.wait_ge(ids_ready, 2)
            nc.vector.memset(rank_item[:, :, ITEMS:ITEMS + 1], 0.0).then_inc(x_added, 1)

            n_last = dve.value_load(ids[0:1, 0:1], min_val=E - 1, max_val=ITEMS - 1)

            def add_item(n, count, column):
                dve.wait_ge(sc_psum, count + 1)
                dve.wait_ge(x_added, count + 1)
                for tb in range(NT):
                    sl = x[:, tb, n * 512:n * 512 + 512]
                    last = nc.vector.scalar_tensor_tensor(sl, (S0, S1)[tb][:], gate_item[:, tb, bass.ds(column, 1)], sl,
                                                          ALU.mult, ALU.add)
                last.then_inc(x_added, 1)

            def item_body(i, last=False):
                def ahead(t):
                    if not last or t + CUT < FFN_TILES:
                        make_lo(dve, T_MOE + t + CUT, i)

                def hidden_lo(j):
                    dve.wait_ge(ht_hi, i * SLABS + PAIRS0 + j + 1)
                    f = lambda t: t[:, 4 * j:4 * j + 4].rearrange("p c t -> p (c t)")
                    lo(f(hTl), T[:], f(hTh), ht_lo)

                def y_cut(n):
                    dve.wait_ge(y_hi, i * 2 + n + 1)
                    sl = slice(n * 512, n * 512 + 512)
                    lo(yl[:, sl], (Y0, Y1)[n][:], yh[:, sl], y_lo)

                for j in range(SLABS):
                    ahead(4 * j)
                    ahead(4 * j + 1)
                    if j == 0:
                        add_item(1, i * 2, i)
                    if j >= 1:
                        hidden_lo(j - 1)
                    if j == 2 and not last:
                        dve.wait_ge(selT_psum, i + 1)
                        pick(i + 1)
                    ahead(4 * j + 2)
                    dve.wait_ge(tile_used, i * FFN_TILES + T_MOE + 4 * j + 4)
                    dve.wait_ge(silu_done, i * SLABS + PAIRS0 + j + 1)
                    dve.wait_ge(ht_psum, i * SLABS + PAIRS0 + j)
                    nc.vector.tensor_tensor(mh, U[:], msilu, ALU.mult).then_inc(h_ready, 1)
                    ahead(4 * j + 3)
                for t in range(DOWN, FFN_TILES):
                    if t == FFN_TILES - 1:
                        y_cut(1)
                    ahead(t)
                    if t == DOWN:
                        hidden_lo(SLABS - 1)
                    if t == DOWN + DT - 1:
                        y_cut(0)
                    if t == DOWN + DT + 4:
                        add_item(0, i * 2 + 1, i + 1)

            with dve.Fori(0, ITEMS - 1) as i:
                with dve.If(i < n_last):
                    item_body(i)
                with dve.Else():
                    dve.nop()
            item_body(n_last, last=True)
            dve.wait_ge(sc_psum, n_last * 2 + 3)
            dve.wait_ge(x_added, n_last * 2 + 3)
            for tb in (1, 0):
                sl = x[:, tb, 512:D]
                nc.vector.scalar_tensor_tensor(sl, (S0, S1)[tb][:], gate_item[:, tb, bass.ds(n_last + 1, 1)], sl,
                                               ALU.mult, ALU.add).then_inc(x_final, 1)
            dve.wait_ge(x_final, 2)
            stats(4)
            dve.wait_ge(c_in[C_GAIN4], 16)
            nc.vector.scalar_tensor_tensor(hn[:, 0], x[:, 0], rstd[:, 0:1], gain[:, 1], ALU.mult,
                                           ALU.mult).then_inc(out_ready[0], 1)


def constants():
    import numpy as np
    pos = np.array([4 * (p % 64) + p // 64 for p in range(S)])
    pool = np.zeros((S, 4, S), np.float32)
    for g, w in enumerate((2, 4, 8, 16)):
        lo = np.clip(pos - w // 2, 0, S)
        hi = np.clip(pos + w - w // 2, 0, S)
        inside = (pos[:, None] >= lo[None]) & (pos[:, None] < hi[None])
        pool[:, g] = inside / (hi - lo)[None].astype(np.float64) - (pos[:, None] == pos[None])
    rel = S - 1 - np.arange(512)
    n = np.abs(rel)
    big = 8 + (np.log(np.maximum(n, 1) / 8.0) / np.log(1024 / 8.0) * 8).astype(np.int32)
    b = np.where(rel > 0, 16, 0) + np.where(n < 8, n, np.minimum(big, 15))
    bucket = (np.arange(32)[:, None] == b[None]).astype(np.float32)
    d = pos[None] - pos[:, None]
    band = np.where(np.abs(d) <= 64, 0.0, BIG).astype(np.float32)
    same = d[:P, :P]
    classes = np.stack([np.where(same % m == 0, 0.0, BIG) for m in (4, 16)]).astype(np.float32)
    tri = np.stack([np.arange(P)[:, None] < np.arange(P)[None], np.ones((P, P))]).astype(np.float32)
    slots = np.where(np.arange(P) < CAP, np.arange(P) + SHIFT, -1.0)
    iota = np.concatenate([slots, np.arange(8)]).astype(np.float32)
    return {"ident": np.eye(P, dtype=np.float32), "pool": pool, "bucket": bucket, "band": band,
            "class": classes, "tri": tri, "iota": iota}


_INS = ["x", "rel_bias", "gains_t", "norm_ffn", "norm_final", "a_w_in", "a_w_group", "a_scale", "a_w_out",
        "b_w_in", "b_w_out", "f_w_gate_up", "f_w_down", "m_router", "m_w_gate_up", "m_w_down"]


def kernel(**inputs):
    import numpy as _np
    import concourse.bacc as _bacc
    from concourse import mybir as _mybir
    from concourse.bass_utils import run_bass_kernel_spmd as _run

    nc = _bacc.Bacc("TRN2", target_bir_lowering=False, num_devices=1, dynamic_dma_scratch_size=128)
    gains = [inputs["norm_mix"][0], inputs["norm_ffn"][0], inputs["norm_mix"][1], inputs["norm_ffn"][1]]
    inputs = dict(inputs, gains_t=_np.stack([_np.asarray(g).reshape(KD, P).T for g in gains], axis=1))
    data = {n: _np.ascontiguousarray(inputs[n]) for n in _INS}
    data["a_scale"] = _np.ascontiguousarray(data["a_scale"].reshape(KD, P).T)
    data.update({f"const_{n}": a for n, a in constants().items()})
    arrays, args = {}, []
    for name, a in data.items():
        arrays[f"in_{name}_dram"] = a
        args.append(nc.dram_tensor(f"in_{name}_dram", a.shape, _mybir.dt.from_np(a.dtype), kind="ExternalInput").ap())
    args.append(nc.dram_tensor("out_0_dram", (1, S, D), _mybir.dt.float32, kind="ExternalOutput").ap())
    encoder(nc, *args)
    r = _run(nc, [arrays], core_ids=[0])
    return r.results[0]["out_0_dram"]
```
